# Optimizing a Trainium2 kernel written in Bass

```python
import jax, jax.numpy as jnp
from jax import lax
import numpy as np

D_MODEL = 1024
BATCH = 1
SEQ = 512
DEPTH = 2

CHUNK = 64
N_MIXERS = 2
CONV_WIDTH = 31
POOL_WINDOWS = (2, 4, 8, 16)
N_POOL_GROUPS = len(POOL_WINDOWS)
GROUP_WIDTH = D_MODEL // N_POOL_GROUPS
D_FF = 4 * D_MODEL
N_CONV_LAYERS = (DEPTH + 1) // 2
N_POOL_LAYERS = DEPTH // 2
EPS = 1e-6

kernel_name = "hybrid_conv_pool_streaming_encoder"

def rmsnorm(x, g):
    xf = x.astype(jnp.float32)
    y = xf * lax.rsqrt(jnp.mean(xf * xf, axis=-1, keepdims=True) + EPS)
    return (y * g.astype(jnp.float32)).astype(x.dtype)

def layernorm(x, g, b):
    xf = x.astype(jnp.float32)
    mu = jnp.mean(xf, axis=-1, keepdims=True)
    var = jnp.mean(jnp.square(xf - mu), axis=-1, keepdims=True)
    y = (xf - mu) * lax.rsqrt(var + EPS)
    return (y * g.astype(jnp.float32) + b.astype(jnp.float32)).astype(x.dtype)

def conformer_conv(h, w1, b1, w_dw, b_dw, ln_g, ln_b, w2, b2):
    u = jnp.einsum('bsd,de->bse', h, w1) + b1
    a, gate = jnp.split(u, 2, axis=-1)
    u = a * jax.nn.sigmoid(gate)
    u = lax.conv_general_dilated(
        u, w_dw[:, None, :].astype(u.dtype),
        window_strides=(1,), padding=[(CONV_WIDTH - 1, 0)],
        dimension_numbers=('NWC', 'WIO', 'NWC'),
        feature_group_count=D_MODEL) + b_dw
    u = jax.nn.silu(layernorm(u, ln_g, ln_b))
    return jnp.einsum('bsd,de->bse', u, w2) + b2

def pool_mixer(h, w_grp, b_grp, scale):
    S = h.shape[1]
    hf = h.astype(jnp.float32)
    cs = jnp.concatenate([jnp.zeros_like(hf[:, :1]), jnp.cumsum(hf, axis=1)], axis=1)
    pos = jnp.arange(S)
    outs = []
    for g, w in enumerate(POOL_WINDOWS):
        sl = slice(g * GROUP_WIDTH, (g + 1) * GROUP_WIDTH)
        lo = jnp.maximum(pos + 1 - w, 0)
        cnt = (pos + 1 - lo).astype(jnp.float32)[None, :, None]
        mean = (cs[:, pos + 1, sl] - cs[:, lo, sl]) / cnt
        outs.append(mean - hf[..., sl])
    p = jnp.concatenate(outs, axis=-1).astype(h.dtype)
    p = p.reshape(p.shape[0], S, N_POOL_GROUPS, GROUP_WIDTH)
    y = jnp.einsum('bsgc,gcd->bsgd', p, w_grp) + b_grp
    return y.reshape(h.shape) * scale

def sqrelu_mlp(h, w1, w2):
    u = jax.nn.relu(jnp.einsum('bsd,df->bsf', h, w1))
    return jnp.einsum('bsf,fd->bsd', u * u, w2)

def setup_inputs(seed: int = 0) -> dict:
    key = jax.random.key(seed)
    ks = jax.random.split(key, 20)
    f = jnp.float32
    D, F, NC, NP, G, GW = D_MODEL, D_FF, N_CONV_LAYERS, N_POOL_LAYERS, N_POOL_GROUPS, GROUP_WIDTH
    nrm = lambda k, s, sc: jax.random.normal(k, s, f) * sc
    return {
        "x": jax.random.normal(ks[0], (BATCH, SEQ, D), f),
        "norm_mix": 1.0 + nrm(ks[1], (DEPTH, D), 0.05),
        "norm_mlp": 1.0 + nrm(ks[2], (DEPTH, D), 0.05),
        "conv_w1": nrm(ks[3], (NC, D, 2 * D), D ** -0.5),
        "conv_b1": nrm(ks[4], (NC, 2 * D), 0.02),
        "conv_dw": nrm(ks[5], (NC, CONV_WIDTH, D), CONV_WIDTH ** -0.5),
        "conv_dwb": nrm(ks[6], (NC, D), 0.02),
        "conv_ln_g": 1.0 + nrm(ks[7], (NC, D), 0.05),
        "conv_ln_b": nrm(ks[8], (NC, D), 0.02),
        "conv_w2": nrm(ks[9], (NC, D, D), D ** -0.5),
        "conv_b2": nrm(ks[10], (NC, D), 0.02),
        "pool_w": nrm(ks[11], (NP, G, GW, GW), GW ** -0.5),
        "pool_b": nrm(ks[12], (NP, G, GW), 0.02),
        "pool_scale": 1.0 + nrm(ks[13], (NP, D), 0.1),
        "mlp_w1": nrm(ks[14], (DEPTH, D, F), D ** -0.5),
        "mlp_w2": nrm(ks[15], (DEPTH, F, D), F ** -0.5),
        "final_norm": 1.0 + nrm(ks[16], (D,), 0.05),
    }

def reference(x, norm_mix, norm_mlp, conv_w1, conv_b1, conv_dw, conv_dwb,
              conv_ln_g, conv_ln_b, conv_w2, conv_b2, pool_w, pool_b,
              pool_scale, mlp_w1, mlp_w2, final_norm):
    h = x
    ic, ip = 0, 0
    for i in range(DEPTH):
        hn = rmsnorm(h, norm_mix[i])
        if i % N_MIXERS == 0:
            mix = conformer_conv(hn, conv_w1[ic], conv_b1[ic], conv_dw[ic], conv_dwb[ic],
                                 conv_ln_g[ic], conv_ln_b[ic], conv_w2[ic], conv_b2[ic])
            ic += 1
        else:
            mix = pool_mixer(hn, pool_w[ip], pool_b[ip], pool_scale[ip])
            ip += 1
        h = h + mix
        h = h + sqrelu_mlp(rmsnorm(h, norm_mlp[i]), mlp_w1[i], mlp_w2[i])
    return rmsnorm(h, final_norm)


_drawn_inputs = setup_inputs


def setup_inputs(seed=0):
    import zlib

    import numpy as np

    out = dict(_drawn_inputs(seed))
    spreads = {}
    factors = {'conv_b1': 4.279, 'conv_ln_b': 5.142, 'conv_b2': 3.128, 'pool_b': 5.183}
    for name, (base, spread) in spreads.items():
        noise = np.random.default_rng([zlib.crc32(name.encode()), seed]).standard_normal(out[name].shape)
        drawn = base * np.exp(spread * noise) if base else spread * noise
        out[name] = __import__('jax').numpy.asarray(drawn.astype(out[name].dtype))
    for name, factor in factors.items():
        out[name] = (out[name] * factor).astype(out[name].dtype)
    return out
```

```python
from contextlib import ExitStack

import concourse.bass as bass
from concourse import mybir

F32 = mybir.dt.float32
F32R = mybir.dt.float32r
BF16 = mybir.dt.bfloat16
ALU = mybir.AluOpType
ACT = mybir.ActivationFunctionType

P = 128
D = 1024
S = 512
F = 4096
NB = S // P
NC = D // P
TAPS = 31
PAD = TAPS - 1
PE_TAPS = 9
NPAR = TAPS + 3
NCUR = NPAR + 2 * PE_TAPS
WINDOWS = (2, 4, 8, 16)
NG = len(WINDOWS)
EPS = 1e-6
GF = 4
GROUPS = F // P // GF
NQ = 2 * NB

GEN_X, GEN_LN, GEN_MLP0, GEN_POOL, GEN_MLP1 = range(5)
NORM_X, NORM_MLP0, NORM_POOL, NORM_MLP1, NORM_OUT = range(5)
Y_MLP = (8, 76)
Y_POOL = 72


def hybrid_encoder(nc, x, norm_mix, norm_mlp, conv_w1, conv_b1, conv_dw, conv_dwb, conv_ln_g, conv_ln_b,
                   conv_w2, conv_b2, pool_w, pool_b, pool_scale, mlp_w1, mlp_w2, final_norm, out):
    ctx = ExitStack()
    with ctx:
        def sb(name, shape, dt=F32):
            return ctx.enter_context(nc.sbuf_tensor(name, shape, dt))

        def sem(name):
            return ctx.enter_context(nc.semaphore(name))

        h = sb("h", [P, NB, D])
        w1_raw = sb("w1_raw", [P, NC * 512])
        w2_raw = sb("w2_raw", [P, GF * D])
        w1_hi = sb("w1_hi", [P, NC * 512], F32R)
        w1_lo = sb("w1_lo", [P, NC * 512], F32R)
        act_hi = sb("act_hi", [P, NC, S], F32R)
        act_lo = sb("act_lo", [P, NC, S], F32R)
        pw_hi = sb("pw_hi", [P, NC, 256], F32R)
        pw_lo = sb("pw_lo", [P, NC, 256], F32R)
        relu = sb("relu", [P, 2, 512])
        spare = relu[:].rearrange("p a b -> p (a b)")
        tok = sb("tok", [P, 2, D])
        gain = sb("gain", [P, 2, D])
        ident = sb("ident", [P, P])
        with ExitStack() as share:
            params = share.enter_context(nc.sbuf_tensor("params", [P, NC, NCUR], F32))
            par = share.enter_context(nc.sbuf_tensor("par", [P, 2, NCUR], F32))
        junk = sb("junk", [P, D], BF16)
        room = sb("room", [P, 32])
        stats = sb("stats", [P, 5, 40])
        rinv = sb("rinv", [P, 40])
        bn = sb("bn", [P, NB, 2, 6])
        moments = sb("moments", [P, NB, 2])
        band = sb("band", [P, NG, P], F32R)
        band0 = sb("band0", [P, NG, P], F32R)
        band_prev = sb("band_prev", [P, NG, 16], F32R)
        inv_first = sb("inv_first", [P, NG, P])
        inv_rest = sb("inv_rest", [P, NG])

        with ExitStack() as share:
            ctok = share.enter_context(nc.sbuf_tensor("ctok", [P, NB, D], F32))
        u_hi = sb("u_hi", [P, GF, S], F32R)
        u_lo = sb("u_lo", [P, GF, S], F32R)
        with ExitStack() as share:
            upad = share.enter_context(nc.sbuf_tensor("upad", [P, 2, PAD + S], F32))
            upad_hi = share.enter_context(nc.sbuf_tensor("upad_hi", [P, 2, PAD + S], F32R))
            upad_lo = share.enter_context(nc.sbuf_tensor("upad_lo", [P, 2, PAD + S], F32R))
            diag_hi = share.enter_context(nc.sbuf_tensor("diag_hi", [P, 2, PE_TAPS, P], F32R))
            diag_lo = share.enter_context(nc.sbuf_tensor("diag_lo", [P, 2, PE_TAPS, P], F32R))
        w2_hi = sb("w2_hi", [P, GF * D], F32R)
        w2_lo = sb("w2_lo", [P, GF * D], F32R)
        ps = ctx.enter_context(nc.psum_tensor("ps", [P, 8, 512], F32))

        cw_raw = w1_raw[:].rearrange("p (s c a f) -> p s c a f", s=2, c=NC, a=2)
        cw_hi = w1_hi[:].rearrange("p (s c a f) -> p s c a f", s=2, c=NC, a=2)
        cw_lo = w1_lo[:].rearrange("p (s c a f) -> p s c a f", s=2, c=NC, a=2)
        m1_raw = w1_raw[:].rearrange("p (c j f) -> p j c f", c=NC, j=GF)
        m1_hi = w1_hi[:].rearrange("p (j c f) -> p j c f", j=GF, c=NC)
        m1_lo = w1_lo[:].rearrange("p (j c f) -> p j c f", j=GF, c=NC)
        m2_raw = w2_raw[:].rearrange("p (f d) -> p f d", f=GF)
        m2_hi = w2_hi[:].rearrange("p (f d) -> p f d", f=GF)
        m2_lo = w2_lo[:].rearrange("p (f d) -> p f d", f=GF)
        c2_hi = (w1_hi[:].rearrange("p (c d) -> p c d", c=NC), w2_hi[:].rearrange("p (c d) -> p c d", c=NC))
        c2_lo = (w1_lo[:].rearrange("p (c d) -> p c d", c=NC), w2_lo[:].rearrange("p (c d) -> p c d", c=NC))
        pt_hi = w1_hi[:].rearrange("p (q d) -> p q d", q=4)
        pt_lo = w1_lo[:].rearrange("p (q d) -> p q d", q=4)
        par_rows = spare[0:NPAR]
        par_r = pw_hi[:, :, 0:PE_TAPS]
        pw_raw = w2_raw[:, 0:NC * 256].rearrange("p (c d) -> p c d", c=NC)
        btmp = ctok[:, 0, 0:NG * P].rearrange("p (g t) -> p g t", g=NG)
        dtmp = ctok[:, 1, 0:NG * P].rearrange("p (g t) -> p g t", g=NG)

        x_in = [sem(f"x_in{b}") for b in range(NB)]
        par_in = sem("par_in")
        gain_in = [sem(f"gain_in{k}") for k in range(2)]
        pb_in = sem("pb_in")
        cw_in = [sem(f"cw_in{k}") for k in range(2)]
        w1_in, w2_in = sem("w1_in"), sem("w2_in")
        stored = [sem(f"stored{k}") for k in range(2)]
        setup, ident_ok, b2_added, c2_lo_ok = sem("setup"), sem("ident_ok"), sem("b2_added"), sem("c2_lo_ok")
        pb_ok, pws_ok, pb_added, band_ok = sem("pb_ok"), sem("pws_ok"), sem("pb_added"), sem("band_ok")
        sq_ok, ms_ok, root_ok = sem("sq_ok"), sem("ms_ok"), sem("root_ok")
        tok_ok = sem("tok_ok")
        turned = sem("turned")
        act_hi_ok, act_lo_ok = sem("act_hi_ok"), sem("act_lo_ok")
        dve_self = sem("dve_self")
        par_t, par_ok, par_hi_ok = sem("par_t"), sem("par_ok"), sem("par_hi_ok")
        cw_hi_ok, cw_lo_ok, glu_mm, sig_ok, glu_ok = (sem(n) for n in ("cw_hi_ok", "cw_lo_ok", "glu_mm", "sig_ok", "glu_ok"))
        up_hi_ok, up_lo_ok, diag_ok, taps_ok = (sem(n) for n in ("up_hi_ok", "up_lo_ok", "diag_ok", "taps_ok"))
        cur_ok, conv_ok, conv_turned, ctok_ok = (sem(n) for n in ("cur_ok", "conv_ok", "conv_turned", "ctok_ok"))
        c2_hi_ok, bn_ok, lnroot_ok, y_ok, swish_sig = (
            sem(n) for n in ("c2_hi_ok", "bn_ok", "lnroot_ok", "y_ok", "swish_sig"))
        y_done, y_added = sem("y_done"), sem("y_added")
        w1_hi_ok, w1_lo_ok, w2_hi_ok, w2_lo_ok = (sem(n) for n in ("w1_hi_ok", "w1_lo_ok", "w2_hi_ok", "w2_lo_ok"))
        up_mm, relu_ok, usq_ok, u_hi_ok, u_lo_ok = (
            sem(n) for n in ("up_mm", "relu_ok", "usq_ok", "u_hi_ok", "u_lo_ok"))
        pt_hi_ok, pt_lo_ok, pooled_ok, pw_hi_ok, pw_lo_ok, out_ok = (
            sem(n) for n in ("pt_hi_ok", "pt_lo_ok", "pooled_ok", "pw_hi_ok", "pw_lo_ok", "out_ok"))

        def col(kind, n, b):
            return stats[:, kind, 4 * n + b:4 * n + b + 1]

        def turn_banks(gen, b):
            first = 4 if gen in (GEN_LN, GEN_POOL, GEN_MLP1) else 0
            lo = first + 2 * (b % 2)
            return ps[:, lo:lo + 2, :].rearrange("p k (c t) -> p (k c) t", t=P)

        def mlp_bank(q):
            return ps[:, 4 + q, :] if q < 4 else ps[:, q - 4, :]

        block = ctx.enter_context(nc.Block())

        @block.sync
        def _(sp):
            def row(src):
                return src.rearrange("(o d) -> o d", o=1).to_broadcast([P, D])

            def load_cw(e, k, s):
                for a in range(2):
                    sp.dma_start(cw_raw[:, s, :, a, :],
                                 conv_w1[0].rearrange("(c p) f -> p c f", p=P)[:, :, bass.ds(e * P + a * D, P)]
                                 ).then_inc(cw_in[s], 16)

            def load_m1(layer, g):
                sp.dma_start(w1_raw[:].rearrange("p (c f) -> p c f", c=NC),
                             mlp_w1[layer].rearrange("(c p) f -> p c f", p=P)[:, :, bass.ds(g * 512, 512)]
                             ).then_inc(w1_in, 16)

            def load_m2(layer, g):
                sp.dma_start(m2_raw,
                             mlp_w2[layer].rearrange("(n p) d -> p n d", p=P)[:, bass.ds(g * GF, GF), :]
                             ).then_inc(w2_in, 16)

            c2_src = conv_w2[0].rearrange("(c p) d -> p c d", p=P)
            for b in range(NB):
                sp.dma_start(h[:, b, :], x[0, b * P:(b + 1) * P, :]).then_inc(x_in[b], 16)
                if b == 0:
                    sp.dma_start(gain[:, 0, :], row(norm_mix[0])).then_inc(gain_in[0], 16)
                    sp.dma_start(par_rows[0:TAPS], conv_dw[0]).then_inc(par_in, 16)
                    sp.dma_start(par_rows[TAPS:TAPS + 1], conv_dwb).then_inc(par_in, 16)
                    sp.dma_start(par_rows[TAPS + 1:TAPS + 3],
                                 conv_b1[0].rearrange("(a d) -> a d", a=2)).then_inc(par_in, 16)
                if b == 1:
                    load_cw(0, 0, 0)
            load_cw(1, 0, 1)
            sp.dma_start(gain[:, 1, :], row(conv_b2[0])).then_inc(gain_in[1], 16)
            sp.dma_start(w2_raw[:].rearrange("p (c d) -> p c d", c=NC), c2_src[:, :, 0:512]).then_inc(w2_in, 16)
            with sp.Fori(0, 3) as i:
                for s in range(2):
                    sp.wait_ge(cw_lo_ok, 2 * i + s + 1)
                    load_cw(2 * i + s + 2, i + 1, s)
            sp.wait_ge(tok_ok, 4)
            sp.dma_start(gain[:, 0, :], row(conv_ln_g[0])).then_inc(gain_in[0], 16)
            sp.wait_ge(b2_added, NB)
            sp.dma_start(gain[:, 1, :], row(conv_ln_b[0])).then_inc(gain_in[1], 16)
            sp.wait_ge(cw_lo_ok, NC)
            sp.dma_start(w1_raw[:].rearrange("p (c d) -> p c d", c=NC), c2_src[:, :, 512:1024]).then_inc(w1_in, 16)
            sp.wait_ge(c2_lo_ok, 1)
            load_m2(0, 0)
            sp.wait_ge(c2_lo_ok, 2)
            load_m1(0, 0)
            sp.wait_ge(y_ok, NB)
            sp.dma_start(gain[:, 0, :], row(norm_mlp[0])).then_inc(gain_in[0], 16)
            sp.dma_start(gain[:, 1, :], row(pool_scale[0])).then_inc(gain_in[1], 16)
            with sp.Fori(0, GROUPS - 1) as g:
                sp.wait_ge(w1_lo_ok, 4 * g + 4)
                load_m1(0, g + 1)
                sp.wait_ge(w2_lo_ok, 4 * g + 4)
                load_m2(0, g + 1)
            sp.dma_start(gain[:, 0, :], row(norm_mix[1])).then_inc(gain_in[0], 16)
            sp.wait_ge(turned, 4 * GEN_MLP0 + NB)
            sp.dma_start(tok[:, 1, :], pool_b[0].rearrange("g d -> (g d)").rearrange("(o d) -> o d", o=1)
                         .to_broadcast([P, D])).then_inc(pb_in, 16)
            sp.wait_ge(w1_lo_ok, 4 * GROUPS)
            load_m1(1, 0)
            sp.wait_ge(w2_lo_ok, 4 * GROUPS)
            sp.dma_start(pw_raw, pool_w[0].rearrange("g (k p) d -> p (g k) d", p=P)).then_inc(w2_in, 16)
            sp.wait_ge(pw_lo_ok, 1)
            load_m2(1, 0)
            sp.wait_ge(pt_lo_ok, NB)
            sp.dma_start(gain[:, 0, :], row(norm_mlp[1])).then_inc(gain_in[0], 16)
            with sp.Fori(0, GROUPS - 1) as g:
                sp.wait_ge(w1_lo_ok, 4 * g + (4 * GROUPS + 4))
                load_m1(1, g + 1)
                sp.wait_ge(w2_lo_ok, 4 * g + (4 * GROUPS + 4))
                load_m2(1, g + 1)
            sp.dma_start(gain[:, 0, :], row(final_norm)).then_inc(gain_in[0], 16)
            for b in range(NB):
                sp.wait_ge(out_ok, b + 1)
                sp.dma_start(out[0, b * P:(b + 1) * P, :], tok[:, b % 2, :]).then_inc(stored[b % 2], 16)
            for k in range(2):
                sp.wait_ge(stored[k], 16 * NB // 2)

        @block.gpsimd
        def _(pool):
            count = [0]

            def link(ins):
                count[0] += 1
                ins.then_inc(setup, 1)
                pool.wait_ge(setup, count[0])

            link(nc.gpsimd.memset(ident[:], 0.0))
            nc.gpsimd.affine_select(out=ident[:], in_=ident[:], compare_op=ALU.not_equal, fill=1.0, base=0,
                                    pattern=[[-1, P]], channel_multiplier=1).then_inc(ident_ok, 1)
            pool.wait_ge(ident_ok, 1)
            link(nc.gpsimd.memset(upad[:, :, 0:PAD], 0.0))
            for b in range(NB):
                pool.wait_ge(tok_ok, b + 1)
                if b == 0:
                    pool.wait_ge(gain_in[1], 16)
                nc.gpsimd.tensor_tensor(h[:, b, :], h[:, b, :], gain[:, 1, :], ALU.add).then_inc(b2_added, 1)
            for g, w in enumerate(WINDOWS):
                link(nc.gpsimd.memset(btmp[:, g, :], 1.0))
                link(nc.gpsimd.affine_select(out=btmp[:, g, :], in_=btmp[:, g, :], compare_op=ALU.is_ge, fill=0.0,
                                             base=0, pattern=[[1, P]], channel_multiplier=-1))
                link(nc.gpsimd.affine_select(out=btmp[:, g, :], in_=btmp[:, g, :], compare_op=ALU.is_ge, fill=0.0,
                                             base=w - 1, pattern=[[-1, P]], channel_multiplier=1))
                link(nc.gpsimd.affine_select(out=btmp[:, g, :], in_=btmp[:, g, :], compare_op=ALU.not_equal,
                                             fill=1.0 - w, base=0, pattern=[[-1, P]], channel_multiplier=1))
                link(nc.gpsimd.iota(dtmp[:, g, :], pattern=[[-1, P]], base=w - 1, channel_multiplier=0,
                                    allow_small_or_imprecise_dtypes=True))
                link(nc.gpsimd.tensor_scalar(dtmp[:, g, :], dtmp[:, g, :], 0.0, None, ALU.max))
                link(nc.gpsimd.tensor_scalar(inv_first[:, g, :], dtmp[:, g, :], -1.0, float(w), ALU.mult, ALU.add))
                link(nc.gpsimd.tensor_tensor(dtmp[:, g, :], dtmp[:, g, :], ident[:], ALU.mult))
                link(nc.gpsimd.memset(inv_rest[:, g:g + 1], 1.0 / w))
            link(nc.gpsimd.tensor_copy(band[:], btmp))
            link(nc.gpsimd.tensor_tensor(band0[:], btmp, dtmp, ALU.add))
            for g, w in enumerate(WINDOWS):
                link(nc.gpsimd.memset(btmp[:, g, 0:16], 1.0))
                link(nc.gpsimd.affine_select(out=btmp[:, g, 0:16], in_=btmp[:, g, 0:16], compare_op=ALU.is_ge,
                                             fill=0.0, base=w - 1 - P, pattern=[[-1, 16]], channel_multiplier=1))
            nc.gpsimd.tensor_copy(band_prev[:], btmp[:, :, 0:16]).then_inc(band_ok, 1)
            pool.wait_ge(c2_hi_ok, 1)
            nc.gpsimd.tensor_tensor(w1_lo[:], w2_raw[:], w1_hi[:], ALU.subtract).then_inc(c2_lo_ok, 1)
            pool.wait_ge(c2_hi_ok, 2)
            nc.gpsimd.tensor_tensor(w2_lo[:], w1_raw[:], w2_hi[:], ALU.subtract).then_inc(c2_lo_ok, 1)
            pool.wait_ge(pb_in, 16)
            pool.wait_ge(gain_in[1], 48)
            nc.gpsimd.tensor_tensor(tok[:, 1, :], tok[:, 1, :], gain[:, 1, :], ALU.mult).then_inc(pb_ok, 1)
            pool.wait_ge(pb_ok, 1)
            pool.wait_ge(w2_in, 16 * (GROUPS + 2))
            scale = gain[:, 1, :].rearrange("p (g d) -> p g d", g=NG)
            for k in range(2):
                v = pw_raw.rearrange("p (g k) d -> p g k d", k=2)[:, :, k, :]
                nc.gpsimd.tensor_tensor(v, v, scale, ALU.mult).then_inc(pws_ok, 1)
            for b in range(NB):
                pool.wait_ge(tok_ok, 4 * GEN_POOL + b + 1)
                nc.gpsimd.tensor_tensor(h[:, b, :], h[:, b, :], tok[:, 1, :], ALU.add).then_inc(pb_added, 1)

        @block.scalar
        def _(act):
            def square(n, b, dst):
                nc.scalar.activation(dst, h[:, b, :], ACT.Square, accum_out=col(0, n, b)).then_inc(sq_ok, 1)

            def root(n, b):
                act.wait_ge(ms_ok, 4 * n + b + 1)
                nc.scalar.activation(col(2, n, b), col(1, n, b), ACT.Sqrt).then_inc(root_ok, 1)

            def act_high(gen, b):
                act.wait_ge(turned, 4 * gen + b + 1)
                nc.scalar.copy(act_hi[:, :, b * P:(b + 1) * P], turn_banks(gen, b)).then_inc(act_hi_ok, 1)

            def cw_high(k, s):
                act.wait_ge(cw_in[s], 32 * k + 32)
                nc.scalar.copy(cw_hi[:, s], cw_raw[:, s]).then_inc(cw_hi_ok, 1)

            for b in range(NB):
                act.wait_ge(x_in[b], 16)
                square(NORM_X, b, ctok[:, 2, :])
                root(NORM_X, b)
                if b >= 1:
                    act_high(GEN_X, b - 1)
                if b == 1:
                    cw_high(0, 0)
            act_high(GEN_X, NB - 1)
            cw_high(0, 1)
            act.wait_ge(par_ok, 1)
            nc.scalar.copy(par_r, params[:, :, 0:PE_TAPS]).then_inc(par_hi_ok, 1)

            def conv_chunk(e, k, s, again, more):
                act.wait_ge(glu_mm, e + 1)
                act.wait_ge(cur_ok, e + 1)
                if again:
                    act.wait_ge(conv_turned, e - 1)
                nc.scalar.activation(relu[:, s, :], ps[:, 2 * s + 1, :], ACT.Sigmoid,
                                     bias=par[:, s, TAPS + 2:TAPS + 3]).then_inc(sig_ok, 1)
                act.wait_ge(glu_ok, e + 1)
                if again:
                    act.wait_ge(taps_ok, e - 1)
                nc.scalar.copy(upad_hi[:, s], upad[:, s]).then_inc(up_hi_ok, 1)
                for t in range(PE_TAPS):
                    nc.scalar.activation(diag_hi[:, s, t], ident[:], ACT.Copy, scale=par[:, s, NPAR + t:NPAR + t + 1])
                    last = nc.scalar.activation(diag_lo[:, s, t], ident[:], ACT.Copy,
                                                scale=par[:, s, NPAR + PE_TAPS + t:NPAR + PE_TAPS + t + 1])
                last.then_inc(diag_ok, 1)
                if more:
                    cw_high(k + 1, s)

            def ctok_copy(e, s):
                act.wait_ge(conv_turned, e + 1)
                nc.scalar.copy(ctok[:, :, bass.ds(e * P, P)],
                               ps[:, 6 + s, :].rearrange("p (b c) -> p b c", b=NB)).then_inc(ctok_ok, 1)

            conv_chunk(0, 0, 0, False, True)
            conv_chunk(1, 0, 1, False, True)
            act.wait_ge(band_ok, 1)
            ctok_copy(0, 0)
            with act.Fori(0, 2) as i:
                for s in range(2):
                    conv_chunk(2 * i + (2 + s), i + 1, s, True, True)
                    ctok_copy(2 * i + (1 + s), 1 - s)
            conv_chunk(6, 3, 0, True, False)
            ctok_copy(5, 1)
            conv_chunk(7, 3, 1, True, False)
            act.wait_ge(w2_in, 16)
            nc.scalar.copy(w1_hi[:], w2_raw[:]).then_inc(c2_hi_ok, 1)
            ctok_copy(6, 0)
            ctok_copy(7, 1)
            act.wait_ge(conv_ok, NC)
            act.wait_ge(taps_ok, NC)
            act.wait_ge(w1_in, 16)
            nc.scalar.copy(w2_hi[:], w1_raw[:]).then_inc(c2_hi_ok, 1)

            act.wait_ge(bn_ok, 1)
            nc.scalar.activation(stats[:, 2, 32:36], stats[:, 1, 32:36], ACT.Sqrt).then_inc(lnroot_ok, 1)
            for b in range(NB):
                act.wait_ge(y_ok, b + 1)
                if b >= 1:
                    act.wait_ge(tok_ok, 4 * GEN_LN + b)
                nc.scalar.activation(spare, tok[:, b % 2, :], ACT.Sigmoid).then_inc(swish_sig, 1)
                if b >= 1:
                    act_high(GEN_LN, b - 1)
            act_high(GEN_LN, NB - 1)

            def w1_high(layer, g, j):
                if j == 0:
                    act.wait_ge(w1_in, 16 * g + (32, 16 * (GROUPS + 2))[layer])
                nc.scalar.copy(m1_hi[:, j], m1_raw[:, j]).then_inc(w1_hi_ok, 1)

            for b in range(NB):
                act.wait_ge(y_added, 5 + b)
                square(NORM_MLP0, b, junk[:])
                root(NORM_MLP0, b)
                if b == 0:
                    act.wait_ge(y_done, NB)
                w1_high(0, 0, b)
                if b >= 2:
                    act_high(GEN_MLP0, b - 2)
            act_high(GEN_MLP0, 2)
            act_high(GEN_MLP0, 3)

            def mlp_up(layer, g):
                for j in range(GF):
                    n = 4 * g + (32 * layer + j)
                    act.wait_ge(up_mm, n + 1)
                    nc.scalar.activation(relu[:, j % 2, :], ps[:, j, :], ACT.Relu).then_inc(relu_ok, 1)
                    if j == 0:
                        act.wait_ge(y_done, 8 * g + Y_MLP[layer])
                        act.wait_ge(w2_in, 16 * g + (32, 16 * (GROUPS + 3))[layer])
                    nc.scalar.copy(m2_hi[:, j], m2_raw[:, j]).then_inc(w2_hi_ok, 1)
                    act.wait_ge(usq_ok, n + 1)
                    nc.scalar.copy(u_hi[:, j], relu[:, j % 2, :]).then_inc(u_hi_ok, 1)

            def mlp_next_w1(layer, g):
                for j in range(GF):
                    act.wait_ge(up_mm, 4 * g + (32 * layer + j - 3))
                    w1_high(layer, g, j)

            with act.Fori(0, GROUPS - 1) as g:
                mlp_up(0, g)
                mlp_next_w1(0, g + 1)
            mlp_up(0, GROUPS - 1)

            def pt_high(b):
                act.wait_ge(tok_ok, 4 * GEN_POOL + b + 1)
                if b == 3:
                    act.wait_ge(turned, 4 * GEN_POOL + 2)
                nc.scalar.copy(pt_hi[:, 1 + b % 3], tok[:, 0, :]).then_inc(pt_hi_ok, 1)

            def pool_high(b):
                act.wait_ge(pooled_ok, b + 1)
                nc.scalar.copy(act_hi[:, :, b * P:(b + 1) * P],
                               spare.rearrange("p (c t) -> p c t", t=P)).then_inc(act_hi_ok, 1)

            for b in range(NB):
                if b >= 1:
                    pt_high(b - 1)
                act.wait_ge(y_added, Y_MLP[0] + 8 * (GROUPS - 1) + 2 * b + 2)
                square(NORM_POOL, b, junk[:])
                if b >= 2:
                    pool_high(b - 2)
                root(NORM_POOL, b)
                if b == 1:
                    act.wait_ge(pws_ok, 2)
                    nc.scalar.copy(pw_hi[:], pw_raw).then_inc(pw_hi_ok, 1)
            pt_high(3)
            w1_high(1, 0, 0)
            pool_high(2)
            for b in range(NB):
                act.wait_ge(y_added, Y_POOL + b + 1)
                square(NORM_MLP1, b, junk[:])
                root(NORM_MLP1, b)
                if b == 0:
                    pool_high(3)
                    act.wait_ge(turned, 4 * GEN_POOL + NB)
                else:
                    act_high(GEN_MLP1, b - 1)
                if b < 3:
                    w1_high(1, 0, b + 1)
            act_high(GEN_MLP1, 3)
            with act.Fori(0, GROUPS - 1) as g:
                mlp_up(1, g)
                mlp_next_w1(1, g + 1)
            mlp_up(1, GROUPS - 1)
            for b in range(NB):
                act.wait_ge(y_added, Y_MLP[1] + 8 * (GROUPS - 1) + 2 * b + 2)
                square(NORM_OUT, b, junk[:])
                root(NORM_OUT, b)

        @block.vector
        def _(dve):
            self_at = [0]

            def link(ins, base=0):
                self_at[0] += 1
                ins.then_inc(dve_self, 1)
                dve.wait_ge(dve_self, base + self_at[0])

            def newton(mean, rt, t, r):
                link(nc.vector.reciprocal(rt, rt))
                link(nc.vector.tensor_tensor(t, rt, rt, ALU.mult))
                link(nc.vector.tensor_tensor(t, t, mean, ALU.mult))
                link(nc.vector.tensor_scalar(t, t, -0.5, 1.5, ALU.mult, ALU.add))
                link(nc.vector.tensor_tensor(r, rt, t, ALU.mult))

            def rms(n, b):
                dve.wait_ge(sq_ok, 4 * n + b + 1)
                nc.vector.tensor_scalar(col(1, n, b), col(0, n, b), 1.0 / D, EPS, ALU.mult, ALU.add).then_inc(ms_ok, 1)
                dve.wait_ge(root_ok, 4 * n + b + 1)
                newton(col(1, n, b), col(2, n, b), col(3, n, b), rinv[:, 4 * n + b:4 * n + b + 1])

            def normed(n, b, dst, done):
                nc.vector.scalar_tensor_tensor(dst, h[:, b, :], rinv[:, 4 * n + b:4 * n + b + 1], gain[:, 0, :],
                                               ALU.mult, ALU.mult).then_inc(done, 1)

            def act_low(gen, b, src=None):
                dve.wait_ge(act_hi_ok, 4 * gen + b + 1)
                at = slice(b * P, (b + 1) * P)
                nc.vector.tensor_tensor(act_lo[:, :, at], turn_banks(gen, b) if src is None else src,
                                        act_hi[:, :, at].bitcast(F32), ALU.subtract).then_inc(act_lo_ok, 1)

            def cw_low(e, s):
                dve.wait_ge(cw_hi_ok, e + 1)
                nc.vector.tensor_tensor(cw_lo[:, s], cw_raw[:, s], cw_hi[:, s].bitcast(F32),
                                        ALU.subtract).then_inc(cw_lo_ok, 1)

            for b in range(NB):
                rms(NORM_X, b)
                if b == 0:
                    dve.wait_ge(gain_in[0], 16)
                if b >= 2:
                    dve.wait_ge(turned, b - 1)
                normed(NORM_X, b, tok[:, b % 2, :], tok_ok)
                if b >= 1:
                    act_low(GEN_X, b - 1)
                if b == 1:
                    cw_low(0, 0)
            act_low(GEN_X, NB - 1)
            cw_low(1, 1)
            dve.wait_ge(par_t, 1)
            nc.vector.tensor_copy(params[:, :, 0:NPAR],
                                  ps[:, 7, 0:NC * NPAR].rearrange("p (c k) -> p c k", c=NC)).then_inc(par_ok, 1)
            dve.wait_ge(par_ok, 1)
            dve.wait_ge(par_hi_ok, 1)
            link(nc.vector.tensor_copy(params[:, :, NPAR:NPAR + PE_TAPS], par_r.bitcast(F32)))
            link(nc.vector.tensor_tensor(params[:, :, NPAR + PE_TAPS:NCUR], params[:, :, 0:PE_TAPS],
                                         par_r.bitcast(F32), ALU.subtract))

            def conv_chunk(e, s, again, more, base=0):
                if again:
                    dve.wait_ge(diag_ok, e - 1)
                nc.vector.tensor_copy(par[:, s, :], params[:, bass.ds(e, 1), :]).then_inc(cur_ok, 1)
                dve.wait_ge(cur_ok, e + 1)
                dve.wait_ge(sig_ok, e + 1)
                if again:
                    dve.wait_ge(up_hi_ok, e - 1)
                nc.vector.scalar_tensor_tensor(upad[:, s, PAD:], ps[:, 2 * s, :], par[:, s, TAPS + 1:TAPS + 2],
                                               relu[:, s, :], ALU.add, ALU.mult).then_inc(glu_ok, 1)
                dve.wait_ge(glu_ok, e + 1)
                t = PE_TAPS
                link(nc.vector.tensor_scalar(relu[:, s, :], upad[:, s, t:t + S], par[:, s, t:t + 1],
                                             par[:, s, TAPS:TAPS + 1], ALU.mult, ALU.add), base)
                dve.wait_ge(up_hi_ok, e + 1)
                nc.vector.tensor_tensor(upad_lo[:, s], upad[:, s], upad_hi[:, s].bitcast(F32),
                                        ALU.subtract).then_inc(up_lo_ok, 1)
                for t in range(PE_TAPS + 1, TAPS):
                    link(nc.vector.scalar_tensor_tensor(relu[:, s, :], upad[:, s, t:t + S], par[:, s, t:t + 1],
                                                        relu[:, s, :], ALU.mult, ALU.add), base)
                    if more and t == PE_TAPS + 4:
                        cw_low(e + 2, s)
                dve.wait_ge(taps_ok, e + 1)
                nc.vector.tensor_tensor(relu[:, s, :], relu[:, s, :], ps[:, 4 + s, :], ALU.add).then_inc(conv_ok, 1)

            dve.wait_ge(setup, 2)
            conv_chunk(0, 0, False, True)
            conv_chunk(1, 1, False, True)
            per_pair = 2 * (TAPS - PE_TAPS)
            with dve.Fori(0, 2) as i:
                for s in range(2):
                    conv_chunk(2 * i + (2 + s), s, True, True, per_pair * i)
            self_at[0] += per_pair
            conv_chunk(6, 0, True, False)
            conv_chunk(7, 1, True, False)

            dve.wait_ge(ctok_ok, NC)
            for b in range(NB):
                nc.vector.bn_stats(bn[:, b, 0, :], ctok[:, b, 0:512])
                link(nc.vector.bn_stats(bn[:, b, 1, :], ctok[:, b, 512:1024]))
                last = nc.vector.bn_aggr(moments[:, b, :], bn[:, b].rearrange("p a k -> p (a k)"))
            link(last)
            ln = slice(32, 36)
            nc.vector.tensor_scalar(stats[:, 1, ln], moments[:, :, 1], 1.0, EPS, ALU.mult, ALU.add).then_inc(bn_ok, 1)
            dve.wait_ge(lnroot_ok, 1)
            newton(stats[:, 1, ln], stats[:, 2, ln], stats[:, 3, ln], rinv[:, ln])

            def swish(b):
                dve.wait_ge(swish_sig, b + 1)
                nc.vector.tensor_tensor(tok[:, b % 2, :], tok[:, b % 2, :], spare, ALU.mult).then_inc(tok_ok, 1)

            dve.wait_ge(gain_in[0], 32)
            dve.wait_ge(gain_in[1], 32)
            for b in range(NB):
                if b >= 2:
                    dve.wait_ge(turned, 4 * GEN_LN + b - 1)
                link(nc.vector.scalar_tensor_tensor(tok[:, b % 2, :], ctok[:, b, :], moments[:, b, 0:1], gain[:, 0, :],
                                                    ALU.subtract, ALU.mult))
                nc.vector.scalar_tensor_tensor(tok[:, b % 2, :], tok[:, b % 2, :], rinv[:, 32 + b:33 + b],
                                               gain[:, 1, :], ALU.mult, ALU.add).then_inc(y_ok, 1)
                if b >= 1:
                    swish(b - 1)
                if b >= 2:
                    act_low(GEN_LN, b - 2)
            swish(3)
            act_low(GEN_LN, 2)
            act_low(GEN_LN, 3)

            def add_tile(n, b, half, bank):
                dve.wait_ge(y_done, n + 1)
                at = h[:, b, half * 512:(half + 1) * 512]
                nc.vector.tensor_tensor(at, at, bank, ALU.add).then_inc(y_added, 1)

            def w1_low(n, j):
                dve.wait_ge(w1_hi_ok, n + 1)
                nc.vector.tensor_tensor(m1_lo[:, j], m1_raw[:, j], m1_hi[:, j].bitcast(F32),
                                        ALU.subtract).then_inc(w1_lo_ok, 1)

            dve.wait_ge(b2_added, NB)
            for b in range(NB):
                add_tile(b, b, 0, ps[:, b, :])
            for b in range(NB):
                add_tile(4 + b, b, 1, ps[:, 4 + b, :])
                rms(NORM_MLP0, b)
                if b == 0:
                    dve.wait_ge(gain_in[0], 48)
                if b >= 2:
                    dve.wait_ge(turned, 4 * GEN_MLP0 + b - 1)
                normed(NORM_MLP0, b, tok[:, b % 2, :], tok_ok)
                w1_low(b, b)
                if b >= 2:
                    act_low(GEN_MLP0, b - 2)
            act_low(GEN_MLP0, 2)
            act_low(GEN_MLP0, 3)
            dve.wait_ge(band_ok, 1)
            nc.vector.reciprocal(inv_first[:], inv_first[:])

            def mlp_up(layer, g):
                for j in range(GF):
                    n = 4 * g + (32 * layer + j)
                    dve.wait_ge(relu_ok, n + 1)
                    nc.vector.tensor_tensor(relu[:, j % 2, :], relu[:, j % 2, :], relu[:, j % 2, :],
                                            ALU.mult).then_inc(usq_ok, 1)
                    dve.wait_ge(w2_hi_ok, n + 1)
                    nc.vector.tensor_tensor(m2_lo[:, j], m2_raw[:, j], m2_hi[:, j].bitcast(F32),
                                            ALU.subtract).then_inc(w2_lo_ok, 1)
                    dve.wait_ge(u_hi_ok, n + 1)
                    nc.vector.tensor_tensor(u_lo[:, j], relu[:, j % 2, :], u_hi[:, j].bitcast(F32),
                                            ALU.subtract).then_inc(u_lo_ok, 1)

            def mlp_add(layer, g, q):
                add_tile(8 * g + (Y_MLP[layer] + q), q // 2, q % 2, mlp_bank(q))

            def mlp_group(layer, g):
                mlp_up(layer, g)
                for q in range(NQ):
                    if q in (0, 2, 4, 6):
                        w1_low(4 * g + (32 * layer + 4 + q // 2), q // 2)
                    mlp_add(layer, g, q)

            with dve.Fori(0, GROUPS - 1) as g:
                mlp_group(0, g)
            mlp_up(0, GROUPS - 1)

            def pt_low(b):
                dve.wait_ge(pt_hi_ok, b + 1)
                nc.vector.tensor_tensor(pt_lo[:, 1 + b % 3], tok[:, 0, :], pt_hi[:, 1 + b % 3].bitcast(F32),
                                        ALU.subtract).then_inc(pt_lo_ok, 1)

            def pooled(b):
                dve.wait_ge(turned, 4 * GEN_POOL + b + 1)
                if b >= 1:
                    dve.wait_ge(act_lo_ok, 4 * GEN_POOL + b)
                if b == 0:
                    for k in range(2):
                        src = turn_banks(GEN_POOL, b).rearrange("p (g k) t -> p g k t", k=2)[:, :, k, :]
                        dst = spare.rearrange("p (g k t) -> p g k t", k=2, t=P)[:, :, k, :]
                        last = nc.vector.tensor_tensor(dst, src, inv_first[:], ALU.mult)
                else:
                    lo = 4 + 2 * (b % 2)
                    last = nc.vector.tensor_tensor(
                        spare.rearrange("p (g c) -> p g c", g=NG),
                        ps[:, lo:lo + 2, :].rearrange("p k (g c) -> p (k g) c", g=2),
                        inv_rest[:].unsqueeze(2).to_broadcast([P, NG, 256]), ALU.mult)
                last.then_inc(pooled_ok, 1)

            def pool_low(b):
                act_low(GEN_POOL, b, spare.rearrange("p (c t) -> p c t", t=P))

            for b in range(NB):
                mlp_add(0, GROUPS - 1, 2 * b)
                mlp_add(0, GROUPS - 1, 2 * b + 1)
                if b >= 1:
                    pt_low(b - 1)
                if b >= 2:
                    pooled(b - 2)
                rms(NORM_POOL, b)
                if b == 0:
                    dve.wait_ge(gain_in[0], 64)
                normed(NORM_POOL, b, tok[:, 0, :], tok_ok)
                if b == 1:
                    dve.wait_ge(pw_hi_ok, 1)
                    nc.vector.tensor_tensor(pw_lo[:], pw_raw, pw_hi[:].bitcast(F32), ALU.subtract).then_inc(pw_lo_ok, 1)
                if b >= 2:
                    pool_low(b - 2)
            pt_low(3)
            w1_low(32, 0)
            pooled(2)
            pool_low(2)

            for b in range(NB):
                dve.wait_ge(y_done, Y_POOL + b + 1)
                dve.wait_ge(pb_added, b + 1)
                lo = 2 * (b % 2)
                at = h[:, b, :].rearrange("p (k d) -> p k d", k=2)
                nc.vector.tensor_tensor(at, at, ps[:, lo:lo + 2, :], ALU.add).then_inc(y_added, 1)
                rms(NORM_MLP1, b)
                if b == 0:
                    dve.wait_ge(gain_in[0], 80)
                if b == 1:
                    dve.wait_ge(pb_added, NB)
                if b >= 2:
                    dve.wait_ge(turned, 4 * GEN_MLP1 + b - 1)
                normed(NORM_MLP1, b, tok[:, b % 2, :], tok_ok)
                if b == 0:
                    pooled(3)
                    pool_low(3)
                else:
                    act_low(GEN_MLP1, b - 1)
                if b < 3:
                    w1_low(33 + b, b + 1)
            act_low(GEN_MLP1, 3)

            with dve.Fori(0, GROUPS - 1) as g:
                mlp_group(1, g)
            mlp_up(1, GROUPS - 1)
            for b in range(NB):
                mlp_add(1, GROUPS - 1, 2 * b)
                mlp_add(1, GROUPS - 1, 2 * b + 1)
                rms(NORM_OUT, b)
                if b == 0:
                    dve.wait_ge(gain_in[0], 96)
                if b >= 2:
                    dve.wait_ge(stored[b % 2], 16)
                normed(NORM_OUT, b, tok[:, b % 2, :], out_ok)

        @block.tensor
        def _(pe):
            def product(dst, left, right, n, count):
                (lh, ll), (rh, rl) = left, right
                nc.tensor.matmul(dst, lh, rh, start=(n == 0), stop=False)
                nc.tensor.matmul(dst, lh, rl, start=False, stop=False)
                return nc.tensor.matmul(dst, ll, rh, start=False, stop=(n == count - 1))

            def act_tile(c, at):
                return act_hi[:, c, at], act_lo[:, c, at]

            def block_cols(b):
                return slice(b * P, (b + 1) * P)

            def turn(gen, b, src):
                pe.wait_ge(tok_ok, 4 * gen + b + 1)
                if b >= 2:
                    pe.wait_ge(act_lo_ok, 4 * gen + b - 1)
                banks = turn_banks(gen, b)
                for c in range(NC):
                    last = nc.tensor.transpose(banks[:, c, :], src[:, c * P:(c + 1) * P], ident[:])
                last.then_inc(turned, 1)

            pe.wait_ge(ident_ok, 1)
            pe.wait_ge(par_in, 48)
            for c in range(NC):
                last = nc.tensor.transpose(ps[:, 7, c * NPAR:(c + 1) * NPAR], par_rows[:, c * P:(c + 1) * P],
                                           ident[0:NPAR, 0:NPAR])
            last.then_inc(par_t, 1)
            for b in range(NB):
                turn(GEN_X, b, tok[:, b % 2, :])

            def glu_product(e, s, again=True):
                pe.wait_ge(cw_lo_ok, e + 1)
                if again:
                    pe.wait_ge(glu_ok, e - 1)
                for a in range(2):
                    for c in range(NC):
                        last = product(ps[:, 2 * s + a, :], (cw_hi[:, s, c, a, :], cw_lo[:, s, c, a, :]),
                                       act_tile(c, slice(0, S)), c, NC)
                last.then_inc(glu_mm, 1)

            def taps(e, s, again):
                pe.wait_ge(diag_ok, e + 1)
                pe.wait_ge(up_lo_ok, e + 1)
                if again:
                    pe.wait_ge(conv_ok, e - 1)
                for t in range(PE_TAPS):
                    last = product(ps[:, 4 + s, :], (diag_hi[:, s, t], diag_lo[:, s, t]),
                                   (upad_hi[:, s, t:t + S], upad_lo[:, s, t:t + S]), t, PE_TAPS)
                last.then_inc(taps_ok, 1)

            def conv_turn(e, s, again=True):
                pe.wait_ge(conv_ok, e + 1)
                if again:
                    pe.wait_ge(ctok_ok, e)
                for b in range(NB):
                    last = nc.tensor.transpose(ps[:, 6 + s, block_cols(b)], relu[:, s, block_cols(b)], ident[:])
                last.then_inc(conv_turned, 1)

            pe.wait_ge(act_lo_ok, NB)
            glu_product(0, 0, False)
            glu_product(1, 1, False)
            taps(0, 0, False)
            glu_product(2, 0)
            taps(1, 1, False)
            conv_turn(0, 0, False)
            with pe.Fori(0, 2) as i:
                for s in range(2):
                    glu_product(2 * i + (3 + s), 1 - s)
                    taps(2 * i + (2 + s), s, True)
                    conv_turn(2 * i + (1 + s), 1 - s)
            glu_product(7, 1)
            taps(6, 0, True)
            conv_turn(5, 1)
            taps(7, 1, True)
            conv_turn(6, 0)
            conv_turn(7, 1)

            def conv_out(b, half, bank):
                for c in range(NC):
                    last = product(ps[:, bank, :], act_tile(c, block_cols(b)), (c2_hi[half][:, c, :], c2_lo[half][:, c, :]),
                                   c, NC)
                last.then_inc(y_done, 1)

            turn(GEN_LN, 0, tok[:, 0, :])
            turn(GEN_LN, 1, tok[:, 1, :])
            for b in range(NB):
                pe.wait_ge(act_lo_ok, 4 * GEN_LN + b + 1)
                if b == 0:
                    pe.wait_ge(c2_lo_ok, 1)
                conv_out(b, 0, b)
                if b < 2:
                    turn(GEN_LN, b + 2, tok[:, b % 2, :])
            pe.wait_ge(c2_lo_ok, 2)
            for b in range(NB):
                conv_out(b, 1, 4 + b)
                if b == 2:
                    turn(GEN_MLP0, 0, tok[:, 0, :])
            for b in range(1, NB):
                turn(GEN_MLP0, b, tok[:, b % 2, :])
            pe.wait_ge(act_lo_ok, 4 * GEN_MLP0 + NB)

            def mlp_up(layer, g):
                for j in range(GF):
                    n = 4 * g + (32 * layer + j)
                    pe.wait_ge(w1_lo_ok, n + 1)
                    pe.wait_ge(y_added, 8 * g + (Y_MLP[layer] - 3 + j))
                    for c in range(NC):
                        last = product(ps[:, j, :], (m1_hi[:, j, c, :], m1_lo[:, j, c, :]), act_tile(c, slice(0, S)), c, NC)
                    last.then_inc(up_mm, 1)

            def down_tile(q, feats, done=False):
                b, half = q // 2, q % 2
                for f in feats:
                    last = product(mlp_bank(q), (u_hi[:, f, block_cols(b)], u_lo[:, f, block_cols(b)]),
                                   (m2_hi[:, f, half * 512:(half + 1) * 512], m2_lo[:, f, half * 512:(half + 1) * 512]), f, GF)
                if done:
                    last.then_inc(y_done, 1)

            def mlp_down(layer, g, between=None):
                n = 4 * g + 32 * layer
                pe.wait_ge(w2_lo_ok, n + 3)
                pe.wait_ge(u_lo_ok, n + 3)
                for q in range(4):
                    down_tile(q, range(GF - 1))
                pe.wait_ge(w2_lo_ok, n + 4)
                pe.wait_ge(u_lo_ok, n + 4)
                for q in range(4):
                    down_tile(q, [GF - 1], True)
                for q in range(4, NQ):
                    down_tile(q, range(GF), True)
                    if q == 5 and between:
                        between()

            with pe.Fori(0, GROUPS - 1) as g:
                mlp_up(0, g)
                mlp_down(0, g)
            mlp_up(0, GROUPS - 1)

            def pool_turn(b):
                pe.wait_ge(pt_lo_ok, b + 1)
                if b >= 2:
                    pe.wait_ge(pooled_ok, b - 1)
                banks = turn_banks(GEN_POOL, b)
                own, before = 1 + b % 3, 1 + (b - 1) % 3
                matrix = band0 if b == 0 else band
                for c in range(NC):
                    g, at = c // 2, slice(c * P, (c + 1) * P)
                    nc.tensor.matmul(banks[:, c, :], pt_hi[:, own, at], matrix[:, g, :], start=True, stop=False)
                    last = nc.tensor.matmul(banks[:, c, :], pt_lo[:, own, at], matrix[:, g, :], start=False, stop=(b == 0))
                    if b:
                        nc.tensor.matmul(banks[:, c, 0:16], pt_hi[:, before, at], band_prev[:, g, :],
                                         start=False, stop=False)
                        last = nc.tensor.matmul(banks[:, c, 0:16], pt_lo[:, before, at], band_prev[:, g, :],
                                                start=False, stop=True)
                last.then_inc(turned, 1)

            def pool_product(b):
                pe.wait_ge(act_lo_ok, 4 * GEN_POOL + b + 1)
                if b == 0:
                    pe.wait_ge(pw_lo_ok, 1)
                    pe.wait_ge(y_added, Y_POOL)
                if b >= 2:
                    pe.wait_ge(y_added, Y_POOL + b - 1)
                for g in range(NG):
                    dst = ps[:, 2 * (b % 2) + g // 2, (g % 2) * 256:(g % 2 + 1) * 256]
                    for k in range(2):
                        last = product(dst, act_tile(2 * g + k, block_cols(b)),
                                       (pw_hi[:, 2 * g + k, :], pw_lo[:, 2 * g + k, :]), k, 2)
                last.then_inc(y_done, 1)

            mlp_down(0, GROUPS - 1, lambda: pool_turn(0))
            pool_turn(1)
            pool_product(0)
            pool_turn(2)
            pool_product(1)
            pool_turn(3)
            pool_product(2)
            turn(GEN_MLP1, 0, tok[:, 0, :])
            pool_product(3)
            for b in range(1, NB):
                turn(GEN_MLP1, b, tok[:, b % 2, :])
            pe.wait_ge(act_lo_ok, 4 * GEN_MLP1 + NB)
            with pe.Fori(0, GROUPS - 1) as g:
                mlp_up(1, g)
                mlp_down(1, g)
            mlp_up(1, GROUPS - 1)
            mlp_down(1, GROUPS - 1)


_INS = ["x", "norm_mix", "norm_mlp", "conv_w1", "conv_b1", "conv_dw", "conv_dwb", "conv_ln_g", "conv_ln_b",
        "conv_w2", "conv_b2", "pool_w", "pool_b", "pool_scale", "mlp_w1", "mlp_w2", "final_norm"]


def kernel(**inputs):
    import numpy as _np
    import concourse.bacc as _bacc
    from concourse import mybir as _mybir
    from concourse.bass_utils import run_bass_kernel_spmd as _run

    nc = _bacc.Bacc("TRN2", target_bir_lowering=False, num_devices=1)
    arrays, args = {}, []
    for name in _INS:
        a = _np.ascontiguousarray(inputs[name])
        arrays[f"in_{name}"] = a
        args.append(nc.dram_tensor(f"in_{name}", a.shape, _mybir.dt.from_np(a.dtype), kind="ExternalInput").ap())
    out = nc.dram_tensor("out", (1, S, D), F32, kind="ExternalOutput").ap()
    hybrid_encoder(nc, *args, out)
    return _run(nc, [arrays], core_ids=[0]).results[0]["out"]
```

```python
from contextlib import ExitStack

import concourse.bass as bass
from concourse import mybir

F32 = mybir.dt.float32
F32R = mybir.dt.float32r
BF16 = mybir.dt.bfloat16
ALU = mybir.AluOpType
ACT = mybir.ActivationFunctionType

P = 128
D = 1024
S = 512
F = 4096
NB = S // P
NC = D // P
TAPS = 31
PAD = TAPS - 1
PE_TAPS = 11
LAST_TAPS = 15
NPAR = TAPS + 3
NCUR = NPAR + 2 * LAST_TAPS
WINDOWS = (2, 4, 8, 16)
NG = len(WINDOWS)
EPS = 1e-6
GF = 4
GROUPS = F // P // GF
NQ = 2 * NB

GEN_X, GEN_LN, GEN_MLP0, GEN_POOL, GEN_MLP1 = range(5)
NORM_X, NORM_MLP0, NORM_POOL, NORM_MLP1, NORM_OUT = range(5)
Y_MLP = (8, 76)
Y_POOL = 72
SQUARES = (0, 4, 12, 20, 24)


def hybrid_encoder(nc, x, norm_mix, norm_mlp, conv_w1, conv_b1, conv_dw, conv_dwb, conv_ln_g, conv_ln_b,
                   conv_w2, conv_b2, pool_w, pool_b, pool_scale, mlp_w1, mlp_w2, final_norm, out):
    ctx = ExitStack()
    with ctx:
        def sb(name, shape, dt=F32):
            return ctx.enter_context(nc.sbuf_tensor(name, shape, dt))

        def sem(name):
            return ctx.enter_context(nc.semaphore(name))

        h = sb("h", [P, NB, D])
        w1_raw = sb("w1_raw", [P, NC * 512])
        w2_raw = sb("w2_raw", [P, GF * D])
        w1_hi = sb("w1_hi", [P, NC * 512], F32R)
        w1_lo = sb("w1_lo", [P, NC * 512], F32R)
        act_hi = sb("act_hi", [P, NC, S], F32R)
        act_lo = sb("act_lo", [P, NC, S], F32R)
        with ExitStack() as share:
            diag_lo = share.enter_context(nc.sbuf_tensor("diag_lo", [P, 2, LAST_TAPS, P], F32R))
        pw_hi = sb("pw_hi", [P, NC, 256], F32R)
        pw_lo = sb("pw_lo", [P, NC, 256], F32R)
        relu = sb("relu", [P, 2, 512])
        spare = relu[:].rearrange("p a b -> p (a b)")
        tok = sb("tok", [P, 2, D])
        gain = sb("gain", [P, 2, D])
        ident = sb("ident", [P, P])
        with ExitStack() as share:
            params = share.enter_context(nc.sbuf_tensor("params", [P, NC, NCUR], F32))
        junk = sb("junk", [P, D], BF16)
        stats = sb("stats", [P, 5, 40])
        rinv = sb("rinv", [P, 40])
        bn = sb("bn", [P, NB, 2, 6])
        moments = sb("moments", [P, NB, 2])
        band = sb("band", [P, NG, P], F32R)
        band0 = sb("band0", [P, NG, P], F32R)
        band_prev = sb("band_prev", [P, NG, 16], F32R)
        inv_first = sb("inv_first", [P, NG, P])

        with ExitStack() as share:
            ctok = share.enter_context(nc.sbuf_tensor("ctok", [P, NB, D], F32))
        u_hi = sb("u_hi", [P, GF, S], F32R)
        u_lo = sb("u_lo", [P, GF, S], F32R)
        with ExitStack() as share:
            upad = share.enter_context(nc.sbuf_tensor("upad", [P, 2, PAD + S], F32))
            upad_hi = share.enter_context(nc.sbuf_tensor("upad_hi", [P, PAD + S], F32R))
            upad_lo = share.enter_context(nc.sbuf_tensor("upad_lo", [P, PAD + S], F32R))
            odd_sum = share.enter_context(nc.sbuf_tensor("odd_sum", [P, S], F32))
            par = share.enter_context(nc.sbuf_tensor("par", [P, 2, NCUR], F32))
            diag_hi = share.enter_context(nc.sbuf_tensor("diag_hi", [P, 2, LAST_TAPS, P], F32R))
        w2_hi = sb("w2_hi", [P, GF * D], F32R)
        w2_lo = sb("w2_lo", [P, GF * D], F32R)
        ps = ctx.enter_context(nc.psum_tensor("ps", [P, 8, 512], F32))

        cw_raw = w1_raw[:].rearrange("p (s c a f) -> p s c a f", s=2, c=NC, a=2)
        cw_hi = w1_hi[:].rearrange("p (s c a f) -> p s c a f", s=2, c=NC, a=2)
        cw_lo = w1_lo[:].rearrange("p (s c a f) -> p s c a f", s=2, c=NC, a=2)
        m1_raw = w1_raw[:].rearrange("p (c j f) -> p j c f", c=NC, j=GF)
        m1_hi = w1_hi[:].rearrange("p (j c f) -> p j c f", j=GF, c=NC)
        m1_lo = w1_lo[:].rearrange("p (j c f) -> p j c f", j=GF, c=NC)
        m2_raw = w2_raw[:].rearrange("p (f d) -> p f d", f=GF)
        m2_hi = w2_hi[:].rearrange("p (f d) -> p f d", f=GF)
        m2_lo = w2_lo[:].rearrange("p (f d) -> p f d", f=GF)
        c2_hi = (w1_hi[:].rearrange("p (c d) -> p c d", c=NC), w2_hi[:].rearrange("p (c d) -> p c d", c=NC))
        c2_lo = (w1_lo[:].rearrange("p (c d) -> p c d", c=NC), w2_lo[:].rearrange("p (c d) -> p c d", c=NC))
        pt_hi = w1_hi[:].rearrange("p (q d) -> p q d", q=4)
        pt_lo = w1_lo[:].rearrange("p (q d) -> p q d", q=4)
        par_rows = spare[0:NPAR]
        par_r = pw_hi[:, :, 0:LAST_TAPS]
        pw_raw = tok[:].rearrange("p a (c d) -> p (a c) d", c=NC // 2)
        btmp = ctok[:, 0, 0:NG * P].rearrange("p (g t) -> p g t", g=NG)
        dtmp = ctok[:, 1, 0:NG * P].rearrange("p (g t) -> p g t", g=NG)

        x_in = [sem(f"x_in{b}") for b in range(NB)]
        par_in = sem("par_in")
        gain_in = [sem(f"gain_in{k}") for k in range(2)]
        pb_in = sem("pb_in")
        cw_in = [sem(f"cw_in{k}") for k in range(2)]
        w1_in, w2_in = sem("w1_in"), sem("w2_in")
        stored = [sem(f"stored{k}") for k in range(2)]
        setup, ident_ok, b2_added, c2_lo_ok = sem("setup"), sem("ident_ok"), sem("b2_added"), sem("c2_lo_ok")
        pb_ok, pws_ok, pb_added, band_ok = sem("pb_ok"), sem("pws_ok"), sem("pb_added"), sem("band_ok")
        pw_in = sem("pw_in")
        sq_ok, ms_ok, root_ok = sem("sq_ok"), sem("ms_ok"), sem("root_ok")
        tok_ok = sem("tok_ok")
        turned = sem("turned")
        act_hi_ok, act_lo_ok = sem("act_hi_ok"), sem("act_lo_ok")
        dve_self, stats_ok = sem("dve_self"), sem("stats_ok")
        par_t, par_ok, par_hi_ok = sem("par_t"), sem("par_ok"), sem("par_hi_ok")
        cw_hi_ok, cw_lo_ok, glu_mm, sig_ok, glu_ok = (sem(n) for n in ("cw_hi_ok", "cw_lo_ok", "glu_mm", "sig_ok", "glu_ok"))
        up_hi_ok, up_lo_ok, diag_ok, taps_ok = (sem(n) for n in ("up_hi_ok", "up_lo_ok", "diag_ok", "taps_ok"))
        diag_more_ok = sem("diag_more_ok")
        cur_ok, conv_ok, conv_turned, ctok_ok = (sem(n) for n in ("cur_ok", "conv_ok", "conv_turned", "ctok_ok"))
        c2_hi_ok, bn_ok, lnroot_ok, y_ok, swish_sig = (
            sem(n) for n in ("c2_hi_ok", "bn_ok", "lnroot_ok", "y_ok", "swish_sig"))
        y_done, y_added = sem("y_done"), sem("y_added")
        w1_hi_ok, w1_lo_ok, w2_hi_ok, w2_lo_ok = (sem(n) for n in ("w1_hi_ok", "w1_lo_ok", "w2_hi_ok", "w2_lo_ok"))
        up_mm, relu_ok, usq_ok, u_hi_ok, u_lo_ok = (
            sem(n) for n in ("up_mm", "relu_ok", "usq_ok", "u_hi_ok", "u_lo_ok"))
        pt_hi_ok, pt_lo_ok, pooled_ok, pw_hi_ok, pw_lo_ok, out_ok = (
            sem(n) for n in ("pt_hi_ok", "pt_lo_ok", "pooled_ok", "pw_hi_ok", "pw_lo_ok", "out_ok"))

        def col(kind, n, b):
            return stats[:, kind, 4 * n + b:4 * n + b + 1]

        def turn_banks(gen, b):
            lo = 2 * b if gen == GEN_MLP0 else 4 + 2 * (b % 2)
            return ps[:, lo:lo + 2, :].rearrange("p k (c t) -> p (k c) t", t=P)

        def mlp_bank(q):
            return ps[:, 4 + q, :] if q < 4 else ps[:, q - 4, :]

        block = ctx.enter_context(nc.Block())

        @block.sync
        def _(sp):
            def row(src):
                return src.rearrange("(o d) -> o d", o=1).to_broadcast([P, D])

            def load_cw(e, k, s):
                for a in range(2):
                    sp.dma_start(cw_raw[:, s, :, a, :],
                                 conv_w1[0].rearrange("(c p) f -> p c f", p=P)[:, :, bass.ds(e * P + a * D, P)]
                                 ).then_inc(cw_in[s], 16)

            def load_m1(layer, g):
                sp.dma_start(w1_raw[:].rearrange("p (c f) -> p c f", c=NC),
                             mlp_w1[layer].rearrange("(c p) f -> p c f", p=P)[:, :, bass.ds(g * 512, 512)]
                             ).then_inc(w1_in, 16)

            def load_m2(layer, g):
                sp.dma_start(m2_raw,
                             mlp_w2[layer].rearrange("(n p) d -> p n d", p=P)[:, bass.ds(g * GF, GF), :]
                             ).then_inc(w2_in, 16)

            c2_src = conv_w2[0].rearrange("(c p) d -> p c d", p=P)
            for b in range(NB):
                sp.dma_start(h[:, b, :], x[0, b * P:(b + 1) * P, :]).then_inc(x_in[b], 16)
                if b == 0:
                    sp.dma_start(gain[:, 0, :], row(norm_mix[0])).then_inc(gain_in[0], 16)
                    sp.dma_start(par_rows[0:TAPS], conv_dw[0]).then_inc(par_in, 16)
                    sp.dma_start(par_rows[TAPS:TAPS + 1], conv_dwb).then_inc(par_in, 16)
                    sp.dma_start(par_rows[TAPS + 1:TAPS + 3],
                                 conv_b1[0].rearrange("(a d) -> a d", a=2)).then_inc(par_in, 16)
                if b == 1:
                    load_cw(0, 0, 0)
            load_cw(1, 0, 1)
            sp.dma_start(gain[:, 1, :], row(conv_b2[0])).then_inc(gain_in[1], 16)
            sp.dma_start(w2_raw[:].rearrange("p (c d) -> p c d", c=NC), c2_src[:, :, 0:512]).then_inc(w2_in, 16)
            with sp.Fori(0, 3) as i:
                for s in range(2):
                    sp.wait_ge(cw_lo_ok, 2 * i + s + 1)
                    load_cw(2 * i + s + 2, i + 1, s)
            sp.wait_ge(tok_ok, 4)
            sp.dma_start(gain[:, 0, :], row(conv_ln_g[0])).then_inc(gain_in[0], 16)
            sp.wait_ge(b2_added, NB)
            sp.dma_start(gain[:, 1, :], row(conv_ln_b[0])).then_inc(gain_in[1], 16)
            sp.wait_ge(cw_lo_ok, NC)
            sp.dma_start(w1_raw[:].rearrange("p (c d) -> p c d", c=NC), c2_src[:, :, 512:1024]).then_inc(w1_in, 16)
            sp.wait_ge(c2_lo_ok, 1)
            load_m2(0, 0)
            sp.wait_ge(c2_lo_ok, 2)
            load_m1(0, 0)
            sp.wait_ge(y_ok, NB)
            sp.dma_start(gain[:, 0, :], row(norm_mlp[0])).then_inc(gain_in[0], 16)
            sp.dma_start(gain[:, 1, :], row(pool_scale[0])).then_inc(gain_in[1], 16)
            sp.wait_ge(turned, 4 * GEN_MLP0 + NB)
            sp.dma_start(pw_raw, pool_w[0].rearrange("g (k p) d -> p (g k) d", p=P)).then_inc(pw_in, 16)
            with sp.Fori(0, GROUPS - 1) as g:
                sp.wait_ge(w1_lo_ok, 4 * g + 4)
                load_m1(0, g + 1)
                sp.wait_ge(w2_lo_ok, 4 * g + 4)
                load_m2(0, g + 1)
            sp.dma_start(gain[:, 0, :], row(norm_mix[1])).then_inc(gain_in[0], 16)
            sp.wait_ge(pw_lo_ok, 1)
            sp.dma_start(tok[:, 1, :], pool_b[0].rearrange("g d -> (g d)").rearrange("(o d) -> o d", o=1)
                         .to_broadcast([P, D])).then_inc(pb_in, 16)
            sp.wait_ge(w1_lo_ok, 4 * GROUPS)
            load_m1(1, 0)
            sp.wait_ge(w2_lo_ok, 4 * GROUPS)
            load_m2(1, 0)
            sp.wait_ge(pt_lo_ok, NB)
            sp.dma_start(gain[:, 0, :], row(norm_mlp[1])).then_inc(gain_in[0], 16)
            with sp.Fori(0, GROUPS - 1) as g:
                sp.wait_ge(w1_lo_ok, 4 * g + (4 * GROUPS + 4))
                load_m1(1, g + 1)
                sp.wait_ge(w2_lo_ok, 4 * g + (4 * GROUPS + 4))
                load_m2(1, g + 1)
            sp.dma_start(gain[:, 0, :], row(final_norm)).then_inc(gain_in[0], 16)
            for b in range(NB):
                for k in range(2):
                    sp.wait_ge(out_ok, 2 * b + k + 1)
                    at = slice(k * 512, (k + 1) * 512)
                    sp.dma_start(out[0, b * P:(b + 1) * P, at], tok[:, b % 2, at]).then_inc(stored[b % 2], 16)
            for k in range(2):
                sp.wait_ge(stored[k], 32 * NB // 2)

        @block.gpsimd
        def _(pool):
            count = [0]

            def link(ins):
                count[0] += 1
                ins.then_inc(setup, 1)
                pool.wait_ge(setup, count[0])

            link(nc.gpsimd.memset(ident[:], 0.0))
            nc.gpsimd.affine_select(out=ident[:], in_=ident[:], compare_op=ALU.not_equal, fill=1.0, base=0,
                                    pattern=[[-1, P]], channel_multiplier=1).then_inc(ident_ok, 1)
            pool.wait_ge(ident_ok, 1)
            link(nc.gpsimd.memset(upad[:, :, 0:PAD], 0.0))
            for b in range(NB):
                pool.wait_ge(tok_ok, b + 1)
                if b == 0:
                    pool.wait_ge(gain_in[1], 16)
                nc.gpsimd.tensor_tensor(h[:, b, :], h[:, b, :], gain[:, 1, :], ALU.add).then_inc(b2_added, 1)
            for g, w in enumerate(WINDOWS):
                link(nc.gpsimd.memset(btmp[:, g, :], 1.0))
                link(nc.gpsimd.affine_select(out=btmp[:, g, :], in_=btmp[:, g, :], compare_op=ALU.is_ge, fill=0.0,
                                             base=0, pattern=[[1, P]], channel_multiplier=-1))
                link(nc.gpsimd.affine_select(out=btmp[:, g, :], in_=btmp[:, g, :], compare_op=ALU.is_ge, fill=0.0,
                                             base=w - 1, pattern=[[-1, P]], channel_multiplier=1))
                link(nc.gpsimd.affine_select(out=btmp[:, g, :], in_=btmp[:, g, :], compare_op=ALU.not_equal,
                                             fill=1.0 - w, base=0, pattern=[[-1, P]], channel_multiplier=1))
                link(nc.gpsimd.iota(dtmp[:, g, :], pattern=[[-1, P]], base=w - 1, channel_multiplier=0,
                                    allow_small_or_imprecise_dtypes=True))
                link(nc.gpsimd.tensor_scalar(dtmp[:, g, :], dtmp[:, g, :], 0.0, None, ALU.max))
                link(nc.gpsimd.tensor_scalar(inv_first[:, g, :], dtmp[:, g, :], -1.0, float(w), ALU.mult, ALU.add))
                link(nc.gpsimd.tensor_tensor(dtmp[:, g, :], dtmp[:, g, :], ident[:], ALU.mult))
            link(nc.gpsimd.tensor_tensor(band0[:], btmp, dtmp, ALU.add))
            for g, w in enumerate(WINDOWS):
                link(nc.gpsimd.tensor_scalar(band[:, g, :], btmp[:, g, :], 1.0 / w, None, ALU.mult))
            for g, w in enumerate(WINDOWS):
                link(nc.gpsimd.memset(btmp[:, g, 0:16], 1.0 / w))
                link(nc.gpsimd.affine_select(out=btmp[:, g, 0:16], in_=btmp[:, g, 0:16], compare_op=ALU.is_ge,
                                             fill=0.0, base=w - 1 - P, pattern=[[-1, 16]], channel_multiplier=1))
            nc.gpsimd.tensor_copy(band_prev[:], btmp[:, :, 0:16]).then_inc(band_ok, 1)
            pool.wait_ge(c2_hi_ok, 1)
            nc.gpsimd.tensor_tensor(w1_lo[:], w2_raw[:], w1_hi[:], ALU.subtract).then_inc(c2_lo_ok, 1)
            pool.wait_ge(c2_hi_ok, 2)
            nc.gpsimd.tensor_tensor(w2_lo[:], w1_raw[:], w2_hi[:], ALU.subtract).then_inc(c2_lo_ok, 1)
            pool.wait_ge(gain_in[1], 48)
            pool.wait_ge(pw_in, 16)
            scale = gain[:, 1, :].rearrange("p (g d) -> p g d", g=NG)
            for k in range(2):
                v = pw_raw.rearrange("p (g k) d -> p g k d", k=2)[:, :, k, :]
                nc.gpsimd.tensor_tensor(v, v, scale, ALU.mult).then_inc(pws_ok, 1)
            pool.wait_ge(pb_in, 16)
            nc.gpsimd.tensor_tensor(tok[:, 1, :], tok[:, 1, :], gain[:, 1, :], ALU.mult).then_inc(pb_ok, 1)
            pool.wait_ge(pb_ok, 1)
            for b in range(NB):
                pool.wait_ge(tok_ok, 4 * GEN_POOL + b + 1)
                nc.gpsimd.tensor_tensor(h[:, b, :], h[:, b, :], tok[:, 1, :], ALU.add).then_inc(pb_added, 1)

        @block.scalar
        def _(act):
            def square(n, b, dst):
                nc.scalar.activation(dst, h[:, b, :], ACT.Square, accum_out=col(0, n, b)).then_inc(sq_ok, 1)

            def square_half(n, b, half, added):
                act.wait_ge(y_added, added)
                at = slice(half * 512, (half + 1) * 512)
                nc.scalar.activation(junk[:, at], h[:, b, at], ACT.Square,
                                     accum_out=col((0, 4)[half], n, b)).then_inc(sq_ok, 1)

            def root(n, b):
                act.wait_ge(ms_ok, 4 * n + b + 1)
                nc.scalar.activation(col(2, n, b), col(1, n, b), ACT.Sqrt, scale=1.0 / D).then_inc(root_ok, 1)

            def act_high(gen, b):
                act.wait_ge(turned, 4 * gen + b + 1)
                nc.scalar.copy(act_hi[:, :, b * P:(b + 1) * P], turn_banks(gen, b)).then_inc(act_hi_ok, 1)

            def cw_high(k, s):
                act.wait_ge(cw_in[s], 32 * k + 32)
                nc.scalar.copy(cw_hi[:, s], cw_raw[:, s]).then_inc(cw_hi_ok, 1)

            act.wait_ge(stats_ok, 1)
            nc.scalar.activation(stats[:, 3, 38:39], stats[:, 4, 38:39], ACT.Sqrt)
            for b in range(NB):
                act.wait_ge(x_in[b], 16)
                square(NORM_X, b, ctok[:, 2, :])
                if b == 2:
                    act_high(GEN_X, 1)
                root(NORM_X, b)
                if b == 1:
                    act.wait_ge(par_ok, 1)
                    nc.scalar.copy(par_r, params[:, :, 0:LAST_TAPS]).then_inc(par_hi_ok, 1)
                if b in (1, 3):
                    act_high(GEN_X, b - 1)
                if b == 1:
                    cw_high(0, 0)
            act_high(GEN_X, NB - 1)
            cw_high(0, 1)

            def diagonals(e, s, again=True, which=range(PE_TAPS), done=diag_ok):
                act.wait_ge(cur_ok, e + 1)
                if again:
                    act.wait_ge(taps_ok, e - 1)
                for t in which:
                    nc.scalar.activation(diag_hi[:, s, t], ident[:], ACT.Copy, scale=par[:, s, NPAR + t:NPAR + t + 1])
                    last = nc.scalar.activation(diag_lo[:, s, t], ident[:], ACT.Copy,
                                                scale=par[:, s, NPAR + LAST_TAPS + t:NPAR + LAST_TAPS + t + 1])
                last.then_inc(done, 1)

            def conv_chunk(e, k, s, again=True, more=True):
                act.wait_ge(cur_ok, e + 1)
                act.wait_ge(glu_mm, e + 1)
                if again:
                    act.wait_ge(conv_turned, e - 1)
                nc.scalar.activation(relu[:, s, :], ps[:, 2 * s + 1, :], ACT.Sigmoid,
                                     bias=par[:, s, TAPS + 2:TAPS + 3]).then_inc(sig_ok, 1)
                act.wait_ge(glu_ok, e + 1)
                if again or s:
                    act.wait_ge(taps_ok, e)
                nc.scalar.copy(upad_hi[:], upad[:, s]).then_inc(up_hi_ok, 1)
                if more:
                    cw_high(k + 1, s)

            def ctok_copy(e, s):
                act.wait_ge(conv_turned, e + 1)
                nc.scalar.copy(ctok[:, :, bass.ds(e * P, P)],
                               ps[:, 6 + s, :].rearrange("p (b c) -> p b c", b=NB)).then_inc(ctok_ok, 1)

            nc.scalar.activation(stats[:, 3, 37:38], ident[:, 0:1], ACT.Sigmoid)
            conv_chunk(0, 0, 0, False)
            diagonals(0, 0, False)
            diagonals(1, 1, False)
            conv_chunk(1, 0, 1, False)
            diagonals(2, 0)
            act.wait_ge(band_ok, 1)
            ctok_copy(0, 0)
            with act.Fori(0, 2) as i:
                for s in range(2):
                    conv_chunk(2 * i + (2 + s), i + 1, s)
                    diagonals(2 * i + (3 + s), 1 - s)
                    ctok_copy(2 * i + (1 + s), 1 - s)
            diagonals(6, 0, True, range(PE_TAPS, LAST_TAPS), diag_more_ok)
            conv_chunk(6, 3, 0, more=False)
            diagonals(7, 1, True, range(LAST_TAPS))
            ctok_copy(5, 1)
            conv_chunk(7, 3, 1, more=False)
            act.wait_ge(w2_in, 16)
            nc.scalar.copy(w1_hi[:], w2_raw[:]).then_inc(c2_hi_ok, 1)
            ctok_copy(6, 0)
            nc.scalar.activation(stats[:, 3, 36:37], ident[:, 0:1], ACT.Sqrt)
            ctok_copy(7, 1)
            act.wait_ge(conv_ok, NC)
            act.wait_ge(taps_ok, NC)
            act.wait_ge(w1_in, 16)
            nc.scalar.copy(w2_hi[:], w1_raw[:]).then_inc(c2_hi_ok, 1)

            act.wait_ge(bn_ok, 1)
            nc.scalar.activation(stats[:, 2, 32:36], stats[:, 1, 32:36], ACT.Sqrt).then_inc(lnroot_ok, 1)
            nc.scalar.activation(stats[:, 3, 37:38], ident[:, 0:1], ACT.Sigmoid)
            for b in range(NB):
                act.wait_ge(y_ok, b + 1)
                if b >= 1:
                    act.wait_ge(tok_ok, 4 * GEN_LN + b)
                nc.scalar.activation(spare, tok[:, b % 2, :], ACT.Sigmoid).then_inc(swish_sig, 1)
                if b >= 1:
                    act_high(GEN_LN, b - 1)
            act_high(GEN_LN, NB - 1)

            def w1_high(layer, g, j):
                if j == 0:
                    act.wait_ge(w1_in, 16 * g + (32, 16 * (GROUPS + 2))[layer])
                nc.scalar.copy(m1_hi[:, j], m1_raw[:, j]).then_inc(w1_hi_ok, 1)

            for b in range(NB):
                square_half(NORM_MLP0, b, 0, 1 + b)
                square_half(NORM_MLP0, b, 1, 5 + b)
                if b >= 1:
                    act_high(GEN_MLP0, b - 1)
                root(NORM_MLP0, b)
                if b == 0:
                    act.wait_ge(y_done, NB)
                if b < 3:
                    w1_high(0, 0, b)
            w1_high(0, 0, 3)
            act_high(GEN_MLP0, 3)

            def mlp_up(layer, g):
                for j in range(GF):
                    n = 4 * g + (32 * layer + j)
                    act.wait_ge(up_mm, n + 1)
                    nc.scalar.activation(relu[:, j % 2, :], ps[:, j, :], ACT.Relu).then_inc(relu_ok, 1)
                    if j == 0:
                        act.wait_ge(y_done, 8 * g + Y_MLP[layer])
                        act.wait_ge(w2_in, 16 * g + (32, 16 * (GROUPS + 2))[layer])
                    nc.scalar.copy(m2_hi[:, j], m2_raw[:, j]).then_inc(w2_hi_ok, 1)
                    act.wait_ge(usq_ok, n + 1)
                    nc.scalar.copy(u_hi[:, j], relu[:, j % 2, :]).then_inc(u_hi_ok, 1)

            def mlp_next_w1(layer, g):
                for j in range(GF):
                    act.wait_ge(up_mm, 4 * g + (32 * layer + j - 3))
                    w1_high(layer, g, j)

            with act.Fori(0, GROUPS - 1) as g:
                mlp_up(0, g)
                mlp_next_w1(0, g + 1)
            act.wait_ge(pws_ok, 2)
            nc.scalar.copy(pw_hi[:], pw_raw).then_inc(pw_hi_ok, 1)
            mlp_up(0, GROUPS - 1)

            def pt_high(b):
                act.wait_ge(tok_ok, 4 * GEN_POOL + b + 1)
                if b == 3:
                    act.wait_ge(turned, 4 * GEN_POOL + 2)
                nc.scalar.copy(pt_hi[:, 1 + b % 3], tok[:, 0, :]).then_inc(pt_hi_ok, 1)

            for b in range(NB):
                if b >= 1:
                    pt_high(b - 1)
                for half in range(2):
                    square_half(NORM_POOL, b, half, Y_MLP[0] + 8 * (GROUPS - 1) + 2 * b + half + 1)
                if b == 2:
                    act.wait_ge(pooled_ok, 1)
                    nc.scalar.copy(act_hi[:, :, 0:P], spare.rearrange("p (c t) -> p c t", t=P)).then_inc(act_hi_ok, 1)
                root(NORM_POOL, b)
                if b == 3:
                    act_high(GEN_POOL, 1)
            pt_high(3)
            act_high(GEN_POOL, 2)
            w1_high(1, 0, 0)
            for b in range(NB):
                act.wait_ge(y_added, Y_POOL + b + 1)
                square(NORM_MLP1, b, junk[:])
                if b == 0:
                    act_high(GEN_POOL, 3)
                if b == 3:
                    act_high(GEN_MLP1, 2)
                root(NORM_MLP1, b)
                if 1 <= b < 3:
                    act_high(GEN_MLP1, b - 1)
                if b == 2:
                    act.wait_ge(turned, 4 * GEN_POOL + NB)
                    w1_high(1, 0, 1)
            w1_high(1, 0, 2)
            w1_high(1, 0, 3)
            act_high(GEN_MLP1, 3)
            with act.Fori(0, GROUPS - 1) as g:
                mlp_up(1, g)
                mlp_next_w1(1, g + 1)
            mlp_up(1, GROUPS - 1)
            for b in range(NB):
                for half in range(2):
                    square_half(NORM_OUT, b, half, Y_MLP[1] + 8 * (GROUPS - 1) + 2 * b + half + 1)
                root(NORM_OUT, b)

        @block.vector
        def _(dve):
            self_at = [0]

            def link(ins, base=0):
                self_at[0] += 1
                ins.then_inc(dve_self, 1)
                dve.wait_ge(dve_self, base + self_at[0])

            def rms(n, b, halves, meanwhile=None):
                total, rt, t = col(1, n, b), col(2, n, b), col(3, n, b)
                if halves:
                    dve.wait_ge(sq_ok, SQUARES[n] + 2 * b + 2)
                    ms = nc.vector.tensor_scalar(total, col(0, n, b), col(4, n, b), D * EPS, ALU.add, ALU.add)
                else:
                    dve.wait_ge(sq_ok, SQUARES[n] + b + 1)
                    ms = nc.vector.tensor_scalar(total, col(0, n, b), D * EPS, None, ALU.add)
                ms.then_inc(ms_ok, 1)
                if meanwhile:
                    meanwhile()
                dve.wait_ge(ms_ok, 4 * n + b + 1)
                dve.wait_ge(root_ok, 4 * n + b + 1)
                link(nc.vector.reciprocal(rt, rt))
                link(nc.vector.scalar_tensor_tensor(t, rt, rt, total, ALU.mult, ALU.mult))
                link(nc.vector.tensor_scalar(t, t, -0.5 / D, 1.5, ALU.mult, ALU.add))
                link(nc.vector.tensor_tensor(rinv[:, 4 * n + b:4 * n + b + 1], rt, t, ALU.mult))

            def normed(n, b, dst, done):
                nc.vector.scalar_tensor_tensor(dst, h[:, b, :], rinv[:, 4 * n + b:4 * n + b + 1], gain[:, 0, :],
                                               ALU.mult, ALU.mult).then_inc(done, 1)

            def act_low(gen, b, src=None):
                dve.wait_ge(act_hi_ok, 4 * gen + b + 1)
                at = slice(b * P, (b + 1) * P)
                nc.vector.tensor_tensor(act_lo[:, :, at], turn_banks(gen, b) if src is None else src,
                                        act_hi[:, :, at].bitcast(F32), ALU.subtract).then_inc(act_lo_ok, 1)

            def cw_low(e, s):
                dve.wait_ge(cw_hi_ok, e + 1)
                nc.vector.tensor_tensor(cw_lo[:, s], cw_raw[:, s], cw_hi[:, s].bitcast(F32),
                                        ALU.subtract).then_inc(cw_lo_ok, 1)

            nc.vector.memset(stats[:, 4, 38:39], 1.0).then_inc(stats_ok, 1)
            for b in range(NB):
                rms(NORM_X, b, False, (lambda: act_low(GEN_X, 2)) if b == 3 else None)
                if b == 0:
                    dve.wait_ge(gain_in[0], 16)
                if b >= 2:
                    dve.wait_ge(turned, b - 1)
                normed(NORM_X, b, tok[:, b % 2, :], tok_ok)
                if b == 0:
                    dve.wait_ge(par_t, 1)
                    nc.vector.tensor_copy(params[:, :, 0:NPAR],
                                          ps[:, 7, 0:NC * NPAR].rearrange("p (c k) -> p c k", c=NC)).then_inc(par_ok, 1)
                if b == 1:
                    act_low(GEN_X, 0)
                    cw_low(0, 0)
                    act_low(GEN_X, 1)
            dve.wait_ge(par_ok, 1)
            dve.wait_ge(par_hi_ok, 1)
            link(nc.vector.tensor_copy(params[:, :, NPAR:NPAR + LAST_TAPS], par_r.bitcast(F32)))
            link(nc.vector.tensor_tensor(params[:, :, NPAR + LAST_TAPS:NCUR], params[:, :, 0:LAST_TAPS],
                                         par_r.bitcast(F32), ALU.subtract))
            act_low(GEN_X, 3)
            cw_low(1, 1)

            def current(e, s, again=True):
                if again:
                    dve.wait_ge(diag_ok, e - 1)
                nc.vector.tensor_copy(par[:, s, :], params[:, bass.ds(e, 1), :]).then_inc(cur_ok, 1)

            def conv_chunk(e, s, again=True, more=True, after=True, base=0, others=PE_TAPS):
                dve.wait_ge(cur_ok, e + 1)
                dve.wait_ge(sig_ok, e + 1)
                nc.vector.scalar_tensor_tensor(upad[:, s, PAD:], ps[:, 2 * s, :], par[:, s, TAPS + 1:TAPS + 2],
                                               relu[:, s, :], ALU.add, ALU.mult).then_inc(glu_ok, 1)
                dve.wait_ge(glu_ok, e + 1)
                sums = (relu[:, s, :], odd_sum[:])
                for n, t in enumerate(range(others, TAPS)):
                    window, weight = upad[:, s, t:t + S], par[:, s, t:t + 1]
                    if n == 2:
                        dve.wait_ge(up_hi_ok, e + 1)
                        nc.vector.tensor_tensor(upad_lo[:], upad[:, s], upad_hi[:].bitcast(F32),
                                                ALU.subtract).then_inc(up_lo_ok, 1)
                    if n >= 2:
                        dve.wait_ge(dve_self, base + (self_at[0] - 1))
                    if n == 0:
                        step = nc.vector.tensor_scalar(sums[0], window, weight, par[:, s, TAPS:TAPS + 1],
                                                       ALU.mult, ALU.add)
                    elif n == 1:
                        step = nc.vector.tensor_scalar(sums[1], window, weight, None, ALU.mult)
                    else:
                        step = nc.vector.scalar_tensor_tensor(sums[n % 2], window, weight, sums[n % 2],
                                                              ALU.mult, ALU.add)
                    self_at[0] += 1
                    step.then_inc(dve_self, 1)
                    if n == 3 and after:
                        current(e + 1, 1 - s, again or s == 1)
                    if n == 8 and more:
                        cw_low(e + 2, s)
                dve.wait_ge(dve_self, base + self_at[0])
                link(nc.vector.tensor_tensor(sums[0], sums[0], sums[1], ALU.add), base)
                dve.wait_ge(taps_ok, e + 1)
                nc.vector.tensor_tensor(sums[0], sums[0], ps[:, 4 + s, :], ALU.add).then_inc(conv_ok, 1)

            dve.wait_ge(setup, 2)
            current(0, 0, False)
            conv_chunk(0, 0, False)
            conv_chunk(1, 1, False)
            per_pair = 2 * (TAPS - PE_TAPS + 1)
            with dve.Fori(0, 2) as i:
                for s in range(2):
                    conv_chunk(2 * i + (2 + s), s, base=per_pair * i)
            self_at[0] += per_pair
            conv_chunk(6, 0, more=False, others=LAST_TAPS)
            conv_chunk(7, 1, more=False, after=False, others=LAST_TAPS)

            for half in range(2):
                dve.wait_ge(ctok_ok, (half + 1) * NC // 2)
                for b in range(NB):
                    last = nc.vector.bn_stats(bn[:, b, half, :], ctok[:, b, half * 512:(half + 1) * 512])
            link(last)
            for b in range(NB):
                last = nc.vector.bn_aggr(moments[:, b, :], bn[:, b].rearrange("p a k -> p (a k)"))
            link(last)
            ln = slice(32, 36)
            nc.vector.tensor_scalar(stats[:, 1, ln], moments[:, :, 1], 1.0, EPS, ALU.mult, ALU.add).then_inc(bn_ok, 1)
            dve.wait_ge(gain_in[0], 32)
            dve.wait_ge(gain_in[1], 32)

            def center(b):
                if b >= 2:
                    dve.wait_ge(turned, 4 * GEN_LN + b - 1)
                link(nc.vector.scalar_tensor_tensor(tok[:, b % 2, :], ctok[:, b, :], moments[:, b, 0:1], gain[:, 0, :],
                                                    ALU.subtract, ALU.mult))

            def swish(b):
                dve.wait_ge(swish_sig, b + 1)
                nc.vector.tensor_tensor(tok[:, b % 2, :], tok[:, b % 2, :], spare, ALU.mult).then_inc(tok_ok, 1)

            center(0)
            rt, t = stats[:, 2, ln], stats[:, 3, ln]
            dve.wait_ge(lnroot_ok, 1)
            link(nc.vector.reciprocal(rt, rt))
            link(nc.vector.tensor_tensor(t, rt, rt, ALU.mult))
            link(nc.vector.tensor_tensor(t, t, stats[:, 1, ln], ALU.mult))
            link(nc.vector.tensor_scalar(t, t, -0.5, 1.5, ALU.mult, ALU.add))
            link(nc.vector.tensor_tensor(rinv[:, ln], rt, t, ALU.mult))
            for b in range(NB):
                nc.vector.scalar_tensor_tensor(tok[:, b % 2, :], tok[:, b % 2, :], rinv[:, 32 + b:33 + b],
                                               gain[:, 1, :], ALU.mult, ALU.add).then_inc(y_ok, 1)
                if b < 3:
                    center(b + 1)
                if b >= 1:
                    act_low(GEN_LN, b - 1)
                swish(b)
            act_low(GEN_LN, 3)

            def add_tile(n, b, half, bank):
                dve.wait_ge(y_done, n + 1)
                at = h[:, b, half * 512:(half + 1) * 512]
                nc.vector.tensor_tensor(at, at, bank, ALU.add).then_inc(y_added, 1)

            def w1_low(n, j):
                dve.wait_ge(w1_hi_ok, n + 1)
                nc.vector.tensor_tensor(m1_lo[:, j], m1_raw[:, j], m1_hi[:, j].bitcast(F32),
                                        ALU.subtract).then_inc(w1_lo_ok, 1)

            dve.wait_ge(b2_added, NB)
            for b in range(NB):
                add_tile(b, b, 0, ps[:, b, :])
            for b in range(NB):
                add_tile(4 + b, b, 1, ps[:, 4 + b, :])
                rms(NORM_MLP0, b, True, (lambda k=b - 1: act_low(GEN_MLP0, k)) if b else None)
                if b == 0:
                    dve.wait_ge(gain_in[0], 48)
                if b >= 2:
                    dve.wait_ge(turned, 4 * GEN_MLP0 + b - 1)
                normed(NORM_MLP0, b, tok[:, b % 2, :], tok_ok)
                if b < 3:
                    w1_low(b, b)
            w1_low(3, 3)
            act_low(GEN_MLP0, 3)
            dve.wait_ge(band_ok, 1)
            nc.vector.reciprocal(inv_first[:], inv_first[:])

            def mlp_up(layer, g):
                for j in range(GF):
                    n = 4 * g + (32 * layer + j)
                    dve.wait_ge(relu_ok, n + 1)
                    nc.vector.tensor_tensor(relu[:, j % 2, :], relu[:, j % 2, :], relu[:, j % 2, :],
                                            ALU.mult).then_inc(usq_ok, 1)
                    dve.wait_ge(w2_hi_ok, n + 1)
                    nc.vector.tensor_tensor(m2_lo[:, j], m2_raw[:, j], m2_hi[:, j].bitcast(F32),
                                            ALU.subtract).then_inc(w2_lo_ok, 1)
                    dve.wait_ge(u_hi_ok, n + 1)
                    nc.vector.tensor_tensor(u_lo[:, j], relu[:, j % 2, :], u_hi[:, j].bitcast(F32),
                                            ALU.subtract).then_inc(u_lo_ok, 1)

            def mlp_add(layer, g, q):
                add_tile(8 * g + (Y_MLP[layer] + q), q // 2, q % 2, mlp_bank(q))

            def mlp_group(layer, g):
                mlp_up(layer, g)
                for q in range(NQ):
                    if q in (0, 2, 4, 6):
                        w1_low(4 * g + (32 * layer + 4 + q // 2), q // 2)
                    mlp_add(layer, g, q)

            with dve.Fori(0, GROUPS - 1) as g:
                mlp_group(0, g)
            dve.wait_ge(pw_hi_ok, 1)
            nc.vector.tensor_tensor(pw_lo[:], pw_raw, pw_hi[:].bitcast(F32), ALU.subtract).then_inc(pw_lo_ok, 1)
            mlp_up(0, GROUPS - 1)

            def pt_low(b):
                dve.wait_ge(pt_hi_ok, b + 1)
                nc.vector.tensor_tensor(pt_lo[:, 1 + b % 3], tok[:, 0, :], pt_hi[:, 1 + b % 3].bitcast(F32),
                                        ALU.subtract).then_inc(pt_lo_ok, 1)

            for b in range(NB):
                mlp_add(0, GROUPS - 1, 2 * b)
                mlp_add(0, GROUPS - 1, 2 * b + 1)
                if b == 2:
                    dve.wait_ge(turned, 4 * GEN_POOL + 1)
                    for k in range(2):
                        src = turn_banks(GEN_POOL, 0).rearrange("p (g k) t -> p g k t", k=2)[:, :, k, :]
                        dst = spare.rearrange("p (g k t) -> p g k t", k=2, t=P)[:, :, k, :]
                        last = nc.vector.tensor_tensor(dst, src, inv_first[:], ALU.mult)
                    last.then_inc(pooled_ok, 1)
                rms(NORM_POOL, b, True, (lambda k=b - 1: pt_low(k)) if b else None)
                if b == 0:
                    dve.wait_ge(gain_in[0], 64)
                else:
                    dve.wait_ge(pt_lo_ok, b)
                normed(NORM_POOL, b, tok[:, 0, :], tok_ok)
                if b == 2:
                    act_low(GEN_POOL, 0, spare.rearrange("p (c t) -> p c t", t=P))
                if b == 3:
                    act_low(GEN_POOL, 1)
            pt_low(3)
            act_low(GEN_POOL, 2)
            w1_low(32, 0)

            def add_pool(b):
                dve.wait_ge(y_done, Y_POOL + b + 1)
                dve.wait_ge(pb_added, b + 1)
                lo = 2 * (b % 2)
                at = h[:, b, :].rearrange("p (k d) -> p k d", k=2)
                nc.vector.tensor_tensor(at, at, ps[:, lo:lo + 2, :], ALU.add).then_inc(y_added, 1)

            def between(b):
                if b == 0:
                    act_low(GEN_POOL, 3)
                if b < 3:
                    add_pool(b + 1)
                else:
                    act_low(GEN_MLP1, 2)

            add_pool(0)
            for b in range(NB):
                rms(NORM_MLP1, b, False, lambda k=b: between(k))
                if b == 0:
                    dve.wait_ge(gain_in[0], 80)
                if b == 1:
                    dve.wait_ge(pb_added, NB)
                if b >= 2:
                    dve.wait_ge(turned, 4 * GEN_MLP1 + b - 1)
                normed(NORM_MLP1, b, tok[:, b % 2, :], tok_ok)
                if 1 <= b < 3:
                    act_low(GEN_MLP1, b - 1)
                if b == 2:
                    w1_low(33, 1)
            w1_low(34, 2)
            w1_low(35, 3)
            act_low(GEN_MLP1, 3)

            with dve.Fori(0, GROUPS - 1) as g:
                mlp_group(1, g)
            mlp_up(1, GROUPS - 1)
            for b in range(NB):
                mlp_add(1, GROUPS - 1, 2 * b)
                mlp_add(1, GROUPS - 1, 2 * b + 1)
                rms(NORM_OUT, b, True)
                if b == 0:
                    dve.wait_ge(gain_in[0], 96)
                if b >= 2:
                    dve.wait_ge(stored[b % 2], 32)
                for k in range(2):
                    at = slice(k * 512, (k + 1) * 512)
                    nc.vector.scalar_tensor_tensor(tok[:, b % 2, at], h[:, b, at], rinv[:, 4 * NORM_OUT + b:4 * NORM_OUT + b + 1],
                                                   gain[:, 0, at], ALU.mult, ALU.mult).then_inc(out_ok, 1)

        @block.tensor
        def _(pe):
            def product(dst, left, right, n, count):
                (lh, ll), (rh, rl) = left, right
                nc.tensor.matmul(dst, lh, rh, start=(n == 0), stop=False)
                nc.tensor.matmul(dst, lh, rl, start=False, stop=False)
                return nc.tensor.matmul(dst, ll, rh, start=False, stop=(n == count - 1))

            def act_tile(c, at):
                return act_hi[:, c, at], act_lo[:, c, at]

            def block_cols(b):
                return slice(b * P, (b + 1) * P)

            def turn(gen, b, src):
                pe.wait_ge(tok_ok, 4 * gen + b + 1)
                if b >= 2:
                    pe.wait_ge(act_lo_ok, 4 * gen + b - 1)
                banks = turn_banks(gen, b)
                for c in range(NC):
                    last = nc.tensor.transpose(banks[:, c, :], src[:, c * P:(c + 1) * P], ident[:])
                last.then_inc(turned, 1)

            pe.wait_ge(ident_ok, 1)
            pe.wait_ge(par_in, 48)
            for c in range(NC):
                last = nc.tensor.transpose(ps[:, 7, c * NPAR:(c + 1) * NPAR], par_rows[:, c * P:(c + 1) * P],
                                           ident[0:NPAR, 0:NPAR])
            last.then_inc(par_t, 1)
            turn(GEN_X, 0, tok[:, 0, :])
            pe.wait_ge(par_ok, 1)
            turn(GEN_X, 1, tok[:, 1, :])

            def glu_product(e, s, again=True):
                pe.wait_ge(cw_lo_ok, e + 1)
                if again:
                    pe.wait_ge(glu_ok, e - 1)
                for a in range(2):
                    for c in range(NC):
                        last = product(ps[:, 2 * s + a, :], (cw_hi[:, s, c, a, :], cw_lo[:, s, c, a, :]),
                                       act_tile(c, slice(0, S)), c, NC)
                last.then_inc(glu_mm, 1)

            def taps(e, s, again, count=PE_TAPS):
                pe.wait_ge(diag_ok, e + 1)
                pe.wait_ge(up_lo_ok, e + 1)
                if again:
                    pe.wait_ge(conv_ok, e - 1)
                for t in range(count):
                    last = product(ps[:, 4 + s, :], (diag_hi[:, s, t], diag_lo[:, s, t]),
                                   (upad_hi[:, t:t + S], upad_lo[:, t:t + S]), t, count)
                last.then_inc(taps_ok, 1)

            def conv_turn(e, s, again=True):
                pe.wait_ge(conv_ok, e + 1)
                if again:
                    pe.wait_ge(ctok_ok, e)
                for b in range(NB):
                    last = nc.tensor.transpose(ps[:, 6 + s, block_cols(b)], relu[:, s, block_cols(b)], ident[:])
                last.then_inc(conv_turned, 1)

            pe.wait_ge(act_lo_ok, 2)
            pe.wait_ge(cw_lo_ok, 1)
            for pair in range(2):
                cols = slice(pair * 2 * P, (pair + 1) * 2 * P)
                if pair:
                    pe.wait_ge(act_lo_ok, NB)
                for a in range(2):
                    for c in range(NC):
                        last = product(ps[:, a, cols], (cw_hi[:, 0, c, a, :], cw_lo[:, 0, c, a, :]),
                                       act_tile(c, cols), c, NC)
                        if pair == 0 and c == NC // 2:
                            turn(GEN_X, 2 + a, tok[:, a, :])
            last.then_inc(glu_mm, 1)
            glu_product(1, 1, False)
            taps(0, 0, False)
            glu_product(2, 0)
            taps(1, 1, False)
            conv_turn(0, 0, False)
            with pe.Fori(0, 2) as i:
                for s in range(2):
                    glu_product(2 * i + (3 + s), 1 - s)
                    taps(2 * i + (2 + s), s, True)
                    conv_turn(2 * i + (1 + s), 1 - s)
            glu_product(7, 1)
            pe.wait_ge(diag_more_ok, 1)
            taps(6, 0, True, LAST_TAPS)
            conv_turn(5, 1)
            taps(7, 1, True, LAST_TAPS)
            conv_turn(6, 0)
            conv_turn(7, 1)

            def conv_out(b, half, bank, between=None):
                for c in range(NC):
                    if c == NC // 4 * (2 - half) and between:
                        between()
                    last = product(ps[:, bank, :], act_tile(c, block_cols(b)), (c2_hi[half][:, c, :], c2_lo[half][:, c, :]),
                                   c, NC)
                last.then_inc(y_done, 1)

            turn(GEN_LN, 0, tok[:, 0, :])
            for b in range(NB):
                pe.wait_ge(act_lo_ok, 4 * GEN_LN + b + 1)
                if b == 0:
                    pe.wait_ge(c2_lo_ok, 1)
                conv_out(b, 0, b, (lambda k=b + 1: turn(GEN_LN, k, tok[:, k % 2, :])) if b < NB - 1 else None)
            pe.wait_ge(c2_lo_ok, 2)
            for b in range(NB):
                conv_out(b, 1, 4 + b, (lambda k=b - 2: turn(GEN_MLP0, k, tok[:, k % 2, :])) if b >= 2 else None)

            def mlp_up(layer, g):
                for j in range(GF):
                    n = 4 * g + (32 * layer + j)
                    pe.wait_ge(w1_lo_ok, n + 1)
                    pe.wait_ge(y_added, 8 * g + (Y_MLP[layer] - 3 + j))
                    for c in range(NC):
                        last = product(ps[:, j, :], (m1_hi[:, j, c, :], m1_lo[:, j, c, :]), act_tile(c, slice(0, S)), c, NC)
                    last.then_inc(up_mm, 1)

            def mlp_up_first(layer, gen):
                for pair in range(2):
                    cols = slice(pair * 2 * P, (pair + 1) * 2 * P)
                    pe.wait_ge(act_lo_ok, 4 * gen + 2 * pair + 2)
                    for j in range(GF):
                        if pair == 0:
                            pe.wait_ge(w1_lo_ok, 32 * layer + j + 1)
                        for c in range(NC):
                            last = product(ps[:, j, cols], (m1_hi[:, j, c, :], m1_lo[:, j, c, :]), act_tile(c, cols), c, NC)
                        if pair:
                            last.then_inc(up_mm, 1)
                        elif j % 2 == 0:
                            turn(gen, 2 + j // 2, tok[:, j // 2, :])

            def down_tile(q, feats, done=False):
                b, half = q // 2, q % 2
                for f in feats:
                    last = product(mlp_bank(q), (u_hi[:, f, block_cols(b)], u_lo[:, f, block_cols(b)]),
                                   (m2_hi[:, f, half * 512:(half + 1) * 512], m2_lo[:, f, half * 512:(half + 1) * 512]), f, GF)
                if done:
                    last.then_inc(y_done, 1)

            def mlp_down(layer, g, between=None):
                n = 4 * g + 32 * layer
                pe.wait_ge(w2_lo_ok, n + 3)
                pe.wait_ge(u_lo_ok, n + 3)
                for q in range(4):
                    down_tile(q, range(GF - 1))
                pe.wait_ge(w2_lo_ok, n + 4)
                pe.wait_ge(u_lo_ok, n + 4)
                for q in range(4):
                    down_tile(q, [GF - 1], True)
                for q in range(4, NQ):
                    down_tile(q, range(GF), True)
                    if q == 5 and between:
                        between()

            mlp_up_first(0, GEN_MLP0)
            mlp_down(0, 0)
            with pe.Fori(1, GROUPS - 1) as g:
                mlp_up(0, g)
                mlp_down(0, g)
            mlp_up(0, GROUPS - 1)

            def pool_turn(b):
                pe.wait_ge(pt_lo_ok, b + 1)
                if b >= 2:
                    pe.wait_ge(act_lo_ok, 4 * GEN_POOL + b - 1)
                banks = turn_banks(GEN_POOL, b)
                own, before = 1 + b % 3, 1 + (b - 1) % 3
                matrix = band0 if b == 0 else band
                for c in range(NC):
                    g, at = c // 2, slice(c * P, (c + 1) * P)
                    nc.tensor.matmul(banks[:, c, :], pt_hi[:, own, at], matrix[:, g, :], start=True, stop=False)
                    last = nc.tensor.matmul(banks[:, c, :], pt_lo[:, own, at], matrix[:, g, :], start=False, stop=(b == 0))
                    if b:
                        nc.tensor.matmul(banks[:, c, 0:16], pt_hi[:, before, at], band_prev[:, g, :],
                                         start=False, stop=False)
                        last = nc.tensor.matmul(banks[:, c, 0:16], pt_lo[:, before, at], band_prev[:, g, :],
                                                start=False, stop=True)
                last.then_inc(turned, 1)

            def pool_product(b):
                pe.wait_ge(act_lo_ok, 4 * GEN_POOL + b + 1)
                if b == 0:
                    pe.wait_ge(pw_lo_ok, 1)
                    pe.wait_ge(y_added, Y_POOL)
                if b >= 2:
                    pe.wait_ge(y_added, Y_POOL + b - 1)
                for g in range(NG):
                    dst = ps[:, 2 * (b % 2) + g // 2, (g % 2) * 256:(g % 2 + 1) * 256]
                    for k in range(2):
                        last = product(dst, act_tile(2 * g + k, block_cols(b)),
                                       (pw_hi[:, 2 * g + k, :], pw_lo[:, 2 * g + k, :]), k, 2)
                last.then_inc(y_done, 1)

            mlp_down(0, GROUPS - 1, lambda: pool_turn(0))
            pool_turn(1)
            pool_product(0)
            pool_turn(2)
            pool_turn(3)
            pool_product(1)
            pool_product(2)
            turn(GEN_MLP1, 0, tok[:, 0, :])
            pool_product(3)
            turn(GEN_MLP1, 1, tok[:, 1, :])
            mlp_up_first(1, GEN_MLP1)
            mlp_down(1, 0)
            with pe.Fori(1, GROUPS - 1) as g:
                mlp_up(1, g)
                mlp_down(1, g)
            mlp_up(1, GROUPS - 1)
            mlp_down(1, GROUPS - 1)


_INS = ["x", "norm_mix", "norm_mlp", "conv_w1", "conv_b1", "conv_dw", "conv_dwb", "conv_ln_g", "conv_ln_b",
        "conv_w2", "conv_b2", "pool_w", "pool_b", "pool_scale", "mlp_w1", "mlp_w2", "final_norm"]


def kernel(**inputs):
    import numpy as _np
    import concourse.bacc as _bacc
    from concourse import mybir as _mybir
    from concourse.bass_utils import run_bass_kernel_spmd as _run

    nc = _bacc.Bacc("TRN2", target_bir_lowering=False, num_devices=1)
    arrays, args = {}, []
    for name in _INS:
        a = _np.ascontiguousarray(inputs[name])
        arrays[f"in_{name}"] = a
        args.append(nc.dram_tensor(f"in_{name}", a.shape, _mybir.dt.from_np(a.dtype), kind="ExternalInput").ap())
    out = nc.dram_tensor("out", (1, S, D), F32, kind="ExternalOutput").ap()
    hybrid_encoder(nc, *args, out)
    return _run(nc, [arrays], core_ids=[0]).results[0]["out"]
```

```python
from contextlib import ExitStack

import concourse.bass as bass
from concourse import mybir

F32 = mybir.dt.float32
F32R = mybir.dt.float32r
BF16 = mybir.dt.bfloat16
ALU = mybir.AluOpType
ACT = mybir.ActivationFunctionType

P = 128
D = 1024
S = 512
F = 4096
NB = S // P
NC = D // P
TAPS = 31
PAD = TAPS - 1
PE_TAPS = 11
LAST_TAPS = 15
NPAR = TAPS + 3
NCUR = NPAR + 2 * LAST_TAPS
WINDOWS = (2, 4, 8, 16)
NG = len(WINDOWS)
EPS = 1e-6
GF = 4
GROUPS = F // P // GF
NQ = 2 * NB

GEN_X, GEN_LN, GEN_MLP0, GEN_POOL, GEN_MLP1 = range(5)
NORM_X, NORM_MLP0, NORM_POOL, NORM_MLP1, NORM_OUT = range(5)
Y_MLP = (8, 76)
Y_POOL = 72
SQUARES = (0, 4, 12, 20, 24)


def hybrid_encoder(nc, x, norm_mix, norm_mlp, conv_w1, conv_b1, conv_dw, conv_dwb, conv_ln_g, conv_ln_b,
                   conv_w2, conv_b2, pool_w, pool_b, pool_scale, mlp_w1, mlp_w2, final_norm, out):
    ctx = ExitStack()
    with ctx:
        def sb(name, shape, dt=F32):
            return ctx.enter_context(nc.sbuf_tensor(name, shape, dt))

        def sem(name):
            return ctx.enter_context(nc.semaphore(name))

        h = sb("h", [P, NB, D])
        w1_raw = sb("w1_raw", [P, NC * 512])
        w2_raw = sb("w2_raw", [P, GF * D])
        w1_hi = sb("w1_hi", [P, NC * 512], F32R)
        w1_lo = sb("w1_lo", [P, NC * 512], F32R)
        act_hi = sb("act_hi", [P, NC, S], F32R)
        act_lo = sb("act_lo", [P, NC, S], F32R)
        with ExitStack() as share:
            diag_lo = share.enter_context(nc.sbuf_tensor("diag_lo", [P, 2, LAST_TAPS, P], F32R))
        with ExitStack() as share:
            band_room = share.enter_context(nc.sbuf_tensor("band_room", [P, 2, NG, P], F32))
        pw_hi = sb("pw_hi", [P, NC, 256], F32R)
        pw_lo = sb("pw_lo", [P, NC, 256], F32R)
        relu = sb("relu", [P, 2, 512])
        spare = relu[:].rearrange("p a b -> p (a b)")
        tok = sb("tok", [P, 2, D])
        gain = sb("gain", [P, 2, D])
        ident = sb("ident", [P, P])
        with ExitStack() as share:
            params = share.enter_context(nc.sbuf_tensor("params", [P, NC, NCUR], F32))
        junk = sb("junk", [P, D], BF16)
        stats = sb("stats", [P, 5, 40])
        rinv = sb("rinv", [P, 40])
        bn = sb("bn", [P, NB, 2, 6])
        moments = sb("moments", [P, NB, 2])
        band = sb("band", [P, NG, P], F32R)
        band0 = sb("band0", [P, NG, P], F32R)
        band_prev = sb("band_prev", [P, NG, 16], F32R)
        inv_first = sb("inv_first", [P, NG, P])

        with ExitStack() as share:
            ctok = share.enter_context(nc.sbuf_tensor("ctok", [P, NB, D], F32))
        u_hi = sb("u_hi", [P, GF, S], F32R)
        u_lo = sb("u_lo", [P, GF, S], F32R)
        with ExitStack() as share:
            upad = share.enter_context(nc.sbuf_tensor("upad", [P, 2, PAD + S], F32))
            upad_hi = share.enter_context(nc.sbuf_tensor("upad_hi", [P, 2, PAD + S], F32R))
            upad_lo = share.enter_context(nc.sbuf_tensor("upad_lo", [P, 2, PAD + S], F32R))
            odd_sum = share.enter_context(nc.sbuf_tensor("odd_sum", [P, S], F32))
            par = share.enter_context(nc.sbuf_tensor("par", [P, 2, NCUR], F32))
            diag_hi = share.enter_context(nc.sbuf_tensor("diag_hi", [P, 2, LAST_TAPS, P], F32R))
        w2_hi = sb("w2_hi", [P, GF * D], F32R)
        w2_lo = sb("w2_lo", [P, GF * D], F32R)
        ps = ctx.enter_context(nc.psum_tensor("ps", [P, 8, 512], F32))

        cw_raw = w1_raw[:].rearrange("p (s c a f) -> p s c a f", s=2, c=NC, a=2)
        cw_hi = w1_hi[:].rearrange("p (s c a f) -> p s c a f", s=2, c=NC, a=2)
        cw_lo = w1_lo[:].rearrange("p (s c a f) -> p s c a f", s=2, c=NC, a=2)
        m1_raw = w1_raw[:].rearrange("p (c j f) -> p j c f", c=NC, j=GF)
        m1_hi = w1_hi[:].rearrange("p (j c f) -> p j c f", j=GF, c=NC)
        m1_lo = w1_lo[:].rearrange("p (j c f) -> p j c f", j=GF, c=NC)
        m2_raw = w2_raw[:].rearrange("p (f d) -> p f d", f=GF)
        m2_hi = w2_hi[:].rearrange("p (f d) -> p f d", f=GF)
        m2_lo = w2_lo[:].rearrange("p (f d) -> p f d", f=GF)
        c2_hi = (w1_hi[:].rearrange("p (c d) -> p c d", c=NC), w2_hi[:].rearrange("p (c d) -> p c d", c=NC))
        c2_lo = (w1_lo[:].rearrange("p (c d) -> p c d", c=NC), w2_lo[:].rearrange("p (c d) -> p c d", c=NC))
        pt_hi = w1_hi[:].rearrange("p (q d) -> p q d", q=4)
        pt_lo = w1_lo[:].rearrange("p (q d) -> p q d", q=4)
        par_rows = spare[0:NPAR]
        par_r = pw_hi[:, :, 0:LAST_TAPS]
        pw_raw = tok[:].rearrange("p a (c d) -> p (a c) d", c=NC // 2)
        b2 = ctok[:, 0, :]
        btmp, dtmp = band_room[:, 0], band_room[:, 1]

        x_in = [sem(f"x_in{b}") for b in range(NB)]
        par_in = sem("par_in")
        gain_in = [sem(f"gain_in{k}") for k in range(2)]
        pb_in = sem("pb_in")
        cw_in = [sem(f"cw_in{k}") for k in range(2)]
        w1_in, w2_in = sem("w1_in"), sem("w2_in")
        stored = [sem(f"stored{k}") for k in range(2)]
        setup, ident_ok, b2_in, c2_lo_ok = sem("setup"), sem("ident_ok"), sem("b2_in"), sem("c2_lo_ok")
        pb_ok, pws_ok, pb_added, band_ok = sem("pb_ok"), sem("pws_ok"), sem("pb_added"), sem("band_ok")
        pw_in = sem("pw_in")
        sq_ok, ms_ok, root_ok = sem("sq_ok"), sem("ms_ok"), sem("root_ok")
        tok_ok = sem("tok_ok")
        turned = sem("turned")
        act_hi_ok, act_lo_ok = sem("act_hi_ok"), sem("act_lo_ok")
        dve_self, stats_ok = sem("dve_self"), sem("stats_ok")
        par_t, par_ok, par_hi_ok = sem("par_t"), sem("par_ok"), sem("par_hi_ok")
        cw_hi_ok, cw_lo_ok, glu_mm, sig_ok, glu_ok = (sem(n) for n in ("cw_hi_ok", "cw_lo_ok", "glu_mm", "sig_ok", "glu_ok"))
        up_hi_ok, up_lo_ok, diag_ok, taps_ok = (sem(n) for n in ("up_hi_ok", "up_lo_ok", "diag_ok", "taps_ok"))
        diag_more_ok = sem("diag_more_ok")
        cur_ok, conv_ok, conv_turned, ctok_ok = (sem(n) for n in ("cur_ok", "conv_ok", "conv_turned", "ctok_ok"))
        c2_hi_ok, bn_ok, lnroot_ok, y_ok, swish_sig = (
            sem(n) for n in ("c2_hi_ok", "bn_ok", "lnroot_ok", "y_ok", "swish_sig"))
        cw_half_hi, cw_half_lo = sem("cw_half_hi"), sem("cw_half_lo")
        y_half, sig_half, tok_half, turned_half, act_half_hi, act_half_lo = (
            sem(n) for n in ("y_half", "sig_half", "tok_half", "turned_half", "act_half_hi", "act_half_lo"))
        y_done, y_added = sem("y_done"), sem("y_added")
        w1_hi_ok, w1_lo_ok, w2_hi_ok, w2_lo_ok = (sem(n) for n in ("w1_hi_ok", "w1_lo_ok", "w2_hi_ok", "w2_lo_ok"))
        up_mm, relu_ok, usq_ok, u_hi_ok, u_lo_ok = (
            sem(n) for n in ("up_mm", "relu_ok", "usq_ok", "u_hi_ok", "u_lo_ok"))
        pt_hi_ok, pt_lo_ok, pooled_ok, pw_hi_ok, pw_lo_ok, out_ok = (
            sem(n) for n in ("pt_hi_ok", "pt_lo_ok", "pooled_ok", "pw_hi_ok", "pw_lo_ok", "out_ok"))

        def col(kind, n, b):
            return stats[:, kind, 4 * n + b:4 * n + b + 1]

        def turn_banks(gen, b):
            lo = 2 * b if gen == GEN_MLP0 else 4 + 2 * (b % 2)
            return ps[:, lo:lo + 2, :].rearrange("p k (c t) -> p (k c) t", t=P)

        def mlp_bank(q):
            return ps[:, 4 + q, :] if q < 4 else ps[:, q - 4, :]

        block = ctx.enter_context(nc.Block())

        @block.sync
        def _(sp):
            def row(src):
                return src.rearrange("(o d) -> o d", o=1).to_broadcast([P, D])

            def load_cw(e, k, s):
                for a in range(2):
                    sp.dma_start(cw_raw[:, s, :, a, :],
                                 conv_w1[0].rearrange("(c p) f -> p c f", p=P)[:, :, bass.ds(e * P + a * D, P)]
                                 ).then_inc(cw_in[s], 16)

            def load_m1(layer, g):
                sp.dma_start(w1_raw[:].rearrange("p (c f) -> p c f", c=NC),
                             mlp_w1[layer].rearrange("(c p) f -> p c f", p=P)[:, :, bass.ds(g * 512, 512)]
                             ).then_inc(w1_in, 16)

            def load_m2(layer, g):
                sp.dma_start(m2_raw,
                             mlp_w2[layer].rearrange("(n p) d -> p n d", p=P)[:, bass.ds(g * GF, GF), :]
                             ).then_inc(w2_in, 16)

            c2_src = conv_w2[0].rearrange("(c p) d -> p c d", p=P)
            for b in range(NB):
                sp.dma_start(h[:, b, :], x[0, b * P:(b + 1) * P, :]).then_inc(x_in[b], 16)
                if b == 0:
                    sp.dma_start(gain[:, 0, :], row(norm_mix[0])).then_inc(gain_in[0], 16)
                    sp.dma_start(par_rows[0:TAPS], conv_dw[0]).then_inc(par_in, 16)
                    sp.dma_start(par_rows[TAPS:TAPS + 1], conv_dwb).then_inc(par_in, 16)
                    sp.dma_start(par_rows[TAPS + 1:TAPS + 3],
                                 conv_b1[0].rearrange("(a d) -> a d", a=2)).then_inc(par_in, 16)
                if b == 1:
                    load_cw(0, 0, 0)
            load_cw(1, 0, 1)
            sp.dma_start(gain[:, 1, :], row(conv_ln_b[0])).then_inc(gain_in[1], 16)
            sp.dma_start(w2_raw[:].rearrange("p (c d) -> p c d", c=NC), c2_src[:, :, 0:512]).then_inc(w2_in, 16)
            with sp.Fori(0, 3) as i:
                for s in range(2):
                    sp.wait_ge(cw_lo_ok, 2 * i + s + 1)
                    load_cw(2 * i + s + 2, i + 1, s)
            sp.wait_ge(tok_ok, 4)
            sp.dma_start(gain[:, 0, :], row(conv_ln_g[0])).then_inc(gain_in[0], 16)
            sp.wait_ge(cw_lo_ok, NC)
            sp.dma_start(w1_raw[:].rearrange("p (c d) -> p c d", c=NC), c2_src[:, :, 512:1024]).then_inc(w1_in, 16)
            sp.wait_ge(c2_lo_ok, 1)
            load_m2(0, 0)
            sp.wait_ge(y_ok, 1)
            sp.dma_start(b2, row(conv_b2[0])).then_inc(b2_in, 16)
            sp.wait_ge(c2_lo_ok, 2)
            load_m1(0, 0)
            sp.wait_ge(y_ok, NB)
            sp.dma_start(gain[:, 0, :], row(norm_mlp[0])).then_inc(gain_in[0], 16)
            sp.dma_start(gain[:, 1, :], row(pool_scale[0])).then_inc(gain_in[1], 16)
            sp.wait_ge(turned, 4 * GEN_MLP0 + NB)
            sp.dma_start(pw_raw, pool_w[0].rearrange("g (k p) d -> p (g k) d", p=P)).then_inc(pw_in, 16)
            with sp.Fori(0, GROUPS - 1) as g:
                sp.wait_ge(w1_lo_ok, 4 * g + 4)
                load_m1(0, g + 1)
                sp.wait_ge(w2_lo_ok, 4 * g + 4)
                load_m2(0, g + 1)
            sp.dma_start(gain[:, 0, :], row(norm_mix[1])).then_inc(gain_in[0], 16)
            sp.wait_ge(pw_lo_ok, 1)
            sp.dma_start(tok[:, 1, :], pool_b[0].rearrange("g d -> (g d)").rearrange("(o d) -> o d", o=1)
                         .to_broadcast([P, D])).then_inc(pb_in, 16)
            sp.wait_ge(w1_lo_ok, 4 * GROUPS)
            load_m1(1, 0)
            sp.wait_ge(w2_lo_ok, 4 * GROUPS)
            load_m2(1, 0)
            sp.wait_ge(pt_lo_ok, NB)
            sp.dma_start(gain[:, 0, :], row(norm_mlp[1])).then_inc(gain_in[0], 16)
            with sp.Fori(0, GROUPS - 1) as g:
                sp.wait_ge(w1_lo_ok, 4 * g + (4 * GROUPS + 4))
                load_m1(1, g + 1)
                sp.wait_ge(w2_lo_ok, 4 * g + (4 * GROUPS + 4))
                load_m2(1, g + 1)
            sp.dma_start(gain[:, 0, :], row(final_norm)).then_inc(gain_in[0], 16)
            for b in range(NB):
                for k in range(2):
                    sp.wait_ge(out_ok, 2 * b + k + 1)
                    at = slice(k * 512, (k + 1) * 512)
                    sp.dma_start(out[0, b * P:(b + 1) * P, at], tok[:, b % 2, at]).then_inc(stored[b % 2], 16)
            for k in range(2):
                sp.wait_ge(stored[k], 32 * NB // 2)

        @block.gpsimd
        def _(pool):
            count = [0]

            def link(ins):
                count[0] += 1
                ins.then_inc(setup, 1)
                pool.wait_ge(setup, count[0])

            link(nc.gpsimd.memset(ident[:], 0.0))
            nc.gpsimd.affine_select(out=ident[:], in_=ident[:], compare_op=ALU.not_equal, fill=1.0, base=0,
                                    pattern=[[-1, P]], channel_multiplier=1).then_inc(ident_ok, 1)
            pool.wait_ge(ident_ok, 1)
            link(nc.gpsimd.memset(upad[:, :, 0:PAD], 0.0))

            def split_c2(lo, raw, hi):
                for k in range(NC):
                    at = slice(k * 512, (k + 1) * 512)
                    last = nc.gpsimd.tensor_tensor(lo[:, at], raw[:, at], hi[:, at], ALU.subtract)
                last.then_inc(c2_lo_ok, 1)

            pool.wait_ge(c2_hi_ok, 1)
            split_c2(w1_lo, w2_raw, w1_hi)
            pool.wait_ge(c2_hi_ok, 2)
            split_c2(w2_lo, w1_raw, w2_hi)
            pool.wait_ge(w1_hi_ok, 1)
            for g, w in enumerate(WINDOWS):
                link(nc.gpsimd.memset(btmp[:, g, :], 1.0))
                link(nc.gpsimd.affine_select(out=btmp[:, g, :], in_=btmp[:, g, :], compare_op=ALU.is_ge, fill=0.0,
                                             base=0, pattern=[[1, P]], channel_multiplier=-1))
                link(nc.gpsimd.affine_select(out=btmp[:, g, :], in_=btmp[:, g, :], compare_op=ALU.is_ge, fill=0.0,
                                             base=w - 1, pattern=[[-1, P]], channel_multiplier=1))
                link(nc.gpsimd.affine_select(out=btmp[:, g, :], in_=btmp[:, g, :], compare_op=ALU.not_equal,
                                             fill=1.0 - w, base=0, pattern=[[-1, P]], channel_multiplier=1))
                link(nc.gpsimd.iota(dtmp[:, g, :], pattern=[[-1, P]], base=w - 1, channel_multiplier=0,
                                    allow_small_or_imprecise_dtypes=True))
                link(nc.gpsimd.tensor_scalar(dtmp[:, g, :], dtmp[:, g, :], 0.0, None, ALU.max))
                link(nc.gpsimd.tensor_scalar(inv_first[:, g, :], dtmp[:, g, :], -1.0, float(w), ALU.mult, ALU.add))
                link(nc.gpsimd.tensor_tensor(dtmp[:, g, :], dtmp[:, g, :], ident[:], ALU.mult))
            link(nc.gpsimd.tensor_tensor(band0[:], btmp, dtmp, ALU.add))
            for g, w in enumerate(WINDOWS):
                link(nc.gpsimd.tensor_scalar(band[:, g, :], btmp[:, g, :], 1.0 / w, None, ALU.mult))
            for g, w in enumerate(WINDOWS):
                link(nc.gpsimd.memset(btmp[:, g, 0:16], 1.0 / w))
                link(nc.gpsimd.affine_select(out=btmp[:, g, 0:16], in_=btmp[:, g, 0:16], compare_op=ALU.is_ge,
                                             fill=0.0, base=w - 1 - P, pattern=[[-1, 16]], channel_multiplier=1))
            nc.gpsimd.tensor_copy(band_prev[:], btmp[:, :, 0:16]).then_inc(band_ok, 1)
            pool.wait_ge(gain_in[1], 32)
            pool.wait_ge(pw_in, 16)
            scale = gain[:, 1, :].rearrange("p (g d) -> p g d", g=NG)
            for k in range(2):
                v = pw_raw.rearrange("p (g k) d -> p g k d", k=2)[:, :, k, :]
                nc.gpsimd.tensor_tensor(v, v, scale, ALU.mult).then_inc(pws_ok, 1)
            pool.wait_ge(pb_in, 16)
            nc.gpsimd.tensor_tensor(tok[:, 1, :], tok[:, 1, :], gain[:, 1, :], ALU.mult).then_inc(pb_ok, 1)
            pool.wait_ge(pb_ok, 1)
            for b in range(NB):
                pool.wait_ge(tok_ok, 4 * GEN_POOL + b + 1)
                nc.gpsimd.tensor_tensor(h[:, b, :], h[:, b, :], tok[:, 1, :], ALU.add).then_inc(pb_added, 1)

        @block.scalar
        def _(act):
            def square(n, b, dst):
                nc.scalar.activation(dst, h[:, b, :], ACT.Square, accum_out=col(0, n, b)).then_inc(sq_ok, 1)

            def square_half(n, b, half, added):
                act.wait_ge(y_added, added)
                at = slice(half * 512, (half + 1) * 512)
                nc.scalar.activation(junk[:, at], h[:, b, at], ACT.Square,
                                     accum_out=col((0, 4)[half], n, b)).then_inc(sq_ok, 1)

            def root(n, b):
                act.wait_ge(ms_ok, 4 * n + b + 1)
                nc.scalar.activation(col(2, n, b), col(1, n, b), ACT.Sqrt, scale=1.0 / D).then_inc(root_ok, 1)

            def act_high(gen, b):
                act.wait_ge(turned, 4 * gen + b + 1)
                nc.scalar.copy(act_hi[:, :, b * P:(b + 1) * P], turn_banks(gen, b)).then_inc(act_hi_ok, 1)

            def cw_high(k, s):
                act.wait_ge(cw_in[s], 32 * k + 32)
                nc.scalar.copy(cw_hi[:, s], cw_raw[:, s]).then_inc(cw_hi_ok, 1)

            def cw_high_half(a, done):
                nc.scalar.copy(cw_hi[:, 0, :, a, :], cw_raw[:, 0, :, a, :]).then_inc(done, 1)

            act.wait_ge(stats_ok, 1)
            nc.scalar.activation(stats[:, 3, 38:39], stats[:, 4, 38:39], ACT.Sqrt)
            for b in range(NB):
                act.wait_ge(x_in[b], 16)
                square(NORM_X, b, ctok[:, 2, :])
                if b == 2:
                    act_high(GEN_X, 1)
                    cw_high_half(1, cw_hi_ok)
                root(NORM_X, b)
                if b == 1:
                    act.wait_ge(par_ok, 1)
                    nc.scalar.copy(par_r, params[:, :, 0:LAST_TAPS]).then_inc(par_hi_ok, 1)
                if b in (1, 3):
                    act_high(GEN_X, b - 1)
                if b == 1:
                    act.wait_ge(cw_in[0], 32)
                    cw_high_half(0, cw_half_hi)
            act_high(GEN_X, NB - 1)
            cw_high(0, 1)

            def diagonals(e, s, again=True, which=range(PE_TAPS), done=diag_ok):
                act.wait_ge(cur_ok, e + 1)
                if again:
                    act.wait_ge(taps_ok, e - 1)
                for t in which:
                    nc.scalar.activation(diag_hi[:, s, t], ident[:], ACT.Copy, scale=par[:, s, NPAR + t:NPAR + t + 1])
                    last = nc.scalar.activation(diag_lo[:, s, t], ident[:], ACT.Copy,
                                                scale=par[:, s, NPAR + LAST_TAPS + t:NPAR + LAST_TAPS + t + 1])
                last.then_inc(done, 1)

            def conv_chunk(e, k, s, again=True, more=True):
                act.wait_ge(cur_ok, e + 1)
                act.wait_ge(glu_mm, e + 1)
                if again:
                    act.wait_ge(conv_turned, e - 1)
                nc.scalar.activation(relu[:, s, :], ps[:, 2 * s + 1, :], ACT.Sigmoid,
                                     bias=par[:, s, TAPS + 2:TAPS + 3]).then_inc(sig_ok, 1)
                act.wait_ge(glu_ok, e + 1)
                if again:
                    act.wait_ge(taps_ok, e - 1)
                nc.scalar.copy(upad_hi[:, s], upad[:, s]).then_inc(up_hi_ok, 1)
                if more:
                    cw_high(k + 1, s)

            def ctok_copy(e, s):
                act.wait_ge(conv_turned, e + 1)
                nc.scalar.copy(ctok[:, :, bass.ds(e * P, P)],
                               ps[:, 6 + s, :].rearrange("p (b c) -> p b c", b=NB)).then_inc(ctok_ok, 1)

            nc.scalar.activation(stats[:, 3, 37:38], ident[:, 0:1], ACT.Sigmoid)
            conv_chunk(0, 0, 0, False)
            diagonals(0, 0, False)
            diagonals(1, 1, False)
            conv_chunk(1, 0, 1, False)
            diagonals(2, 0)
            ctok_copy(0, 0)
            with act.Fori(0, 2) as i:
                for s in range(2):
                    conv_chunk(2 * i + (2 + s), i + 1, s)
                    diagonals(2 * i + (3 + s), 1 - s)
                    ctok_copy(2 * i + (1 + s), 1 - s)
            diagonals(6, 0, True, range(PE_TAPS, LAST_TAPS), diag_more_ok)
            conv_chunk(6, 3, 0, more=False)
            diagonals(7, 1, True, range(LAST_TAPS))
            ctok_copy(5, 1)
            conv_chunk(7, 3, 1, more=False)
            act.wait_ge(w2_in, 16)
            nc.scalar.copy(w1_hi[:], w2_raw[:]).then_inc(c2_hi_ok, 1)
            ctok_copy(6, 0)
            nc.scalar.activation(stats[:, 3, 36:37], ident[:, 0:1], ACT.Sqrt)
            ctok_copy(7, 1)
            act.wait_ge(conv_ok, NC)
            act.wait_ge(taps_ok, NC)
            act.wait_ge(w1_in, 16)
            nc.scalar.copy(w2_hi[:], w1_raw[:]).then_inc(c2_hi_ok, 1)

            act.wait_ge(bn_ok, 1)
            nc.scalar.activation(stats[:, 2, 32:36], stats[:, 1, 32:36], ACT.Sqrt).then_inc(lnroot_ok, 1)
            nc.scalar.activation(stats[:, 3, 37:38], ident[:, 0:1], ACT.Sigmoid)
            low, high = slice(0, 512), slice(512, 1024)
            act.wait_ge(y_half, 1)
            nc.scalar.activation(spare[:, low], tok[:, 0, low], ACT.Sigmoid).then_inc(sig_half, 1)
            act.wait_ge(y_ok, 1)
            nc.scalar.activation(spare[:, high], tok[:, 0, high], ACT.Sigmoid).then_inc(swish_sig, 1)
            banks = turn_banks(GEN_LN, 0)
            act.wait_ge(turned_half, 1)
            nc.scalar.copy(act_hi[:, 0:NC // 2, 0:P], banks[:, 0:NC // 2]).then_inc(act_half_hi, 1)
            act.wait_ge(turned, 4 * GEN_LN + 1)
            nc.scalar.copy(act_hi[:, NC // 2:, 0:P], banks[:, NC // 2:]).then_inc(act_hi_ok, 1)
            for b in range(1, NB):
                if b >= 2:
                    act_high(GEN_LN, b - 1)
                act.wait_ge(y_ok, b + 1)
                act.wait_ge(tok_ok, 4 * GEN_LN + b)
                nc.scalar.activation(spare, tok[:, b % 2, :], ACT.Sigmoid).then_inc(swish_sig, 1)
            act_high(GEN_LN, NB - 1)

            def w1_high(layer, g, j):
                if j == 0:
                    act.wait_ge(w1_in, 16 * g + (32, 16 * (GROUPS + 2))[layer])
                nc.scalar.copy(m1_hi[:, j], m1_raw[:, j]).then_inc(w1_hi_ok, 1)

            for b in range(NB):
                square_half(NORM_MLP0, b, 0, 1 + b)
                square_half(NORM_MLP0, b, 1, 5 + b)
                if b >= 1:
                    act_high(GEN_MLP0, b - 1)
                root(NORM_MLP0, b)
                if b == 0:
                    act.wait_ge(y_done, NB)
                if b < 3:
                    w1_high(0, 0, b)
            w1_high(0, 0, 3)
            act_high(GEN_MLP0, 3)

            def w2_high(layer, g, j):
                if j == 0:
                    act.wait_ge(y_done, 8 * g + Y_MLP[layer])
                    act.wait_ge(w2_in, 16 * g + (32, 16 * (GROUPS + 2))[layer])
                nc.scalar.copy(m2_hi[:, j], m2_raw[:, j]).then_inc(w2_hi_ok, 1)

            def mlp_up(layer, g, first=False):
                if first:
                    for j in range(GF):
                        w2_high(layer, g, j)
                for j in range(GF):
                    n = 4 * g + (32 * layer + j)
                    act.wait_ge(up_mm, n + 1)
                    nc.scalar.activation(relu[:, j % 2, :], ps[:, j, :], ACT.Relu).then_inc(relu_ok, 1)
                    if not first:
                        w2_high(layer, g, j)
                    act.wait_ge(usq_ok, n + 1)
                    nc.scalar.copy(u_hi[:, j], relu[:, j % 2, :]).then_inc(u_hi_ok, 1)

            def mlp_next_w1(layer, g):
                for j in range(GF):
                    act.wait_ge(up_mm, 4 * g + (32 * layer + j - 3))
                    w1_high(layer, g, j)

            mlp_up(0, 0, True)
            mlp_next_w1(0, 1)
            with act.Fori(1, GROUPS - 1) as g:
                mlp_up(0, g)
                mlp_next_w1(0, g + 1)
            act.wait_ge(pws_ok, 2)
            nc.scalar.copy(pw_hi[:], pw_raw).then_inc(pw_hi_ok, 1)
            mlp_up(0, GROUPS - 1)

            act.wait_ge(up_mm, 4 * GROUPS)
            w1_high(1, 0, 0)
            def pt_high(b):
                act.wait_ge(tok_ok, 4 * GEN_POOL + b + 1)
                if b == 3:
                    act.wait_ge(turned, 4 * GEN_POOL + 2)
                nc.scalar.copy(pt_hi[:, 1 + b % 3], tok[:, 0, :]).then_inc(pt_hi_ok, 1)

            for b in range(NB):
                if b >= 1:
                    pt_high(b - 1)
                for half in range(2):
                    square_half(NORM_POOL, b, half, Y_MLP[0] + 8 * (GROUPS - 1) + 2 * b + half + 1)
                if b == 2:
                    act.wait_ge(pooled_ok, 1)
                    nc.scalar.copy(act_hi[:, :, 0:P], spare.rearrange("p (c t) -> p c t", t=P)).then_inc(act_hi_ok, 1)
                root(NORM_POOL, b)
                if b == 3:
                    act_high(GEN_POOL, 1)
            pt_high(3)
            act_high(GEN_POOL, 2)
            for b in range(NB):
                act.wait_ge(y_added, Y_POOL + b + 1)
                square(NORM_MLP1, b, junk[:])
                root(NORM_MLP1, b)
                if b == 0:
                    act_high(GEN_POOL, 3)
                if 1 <= b < 3:
                    act_high(GEN_MLP1, b - 1)
                if b == 2:
                    act.wait_ge(turned, 4 * GEN_POOL + NB)
                    w1_high(1, 0, 1)
            w1_high(1, 0, 2)
            w1_high(1, 0, 3)
            act_high(GEN_MLP1, 2)
            act_high(GEN_MLP1, 3)
            mlp_up(1, 0, True)
            mlp_next_w1(1, 1)
            with act.Fori(1, GROUPS - 1) as g:
                mlp_up(1, g)
                mlp_next_w1(1, g + 1)
            mlp_up(1, GROUPS - 1)
            for b in range(NB):
                for half in range(2):
                    square_half(NORM_OUT, b, half, Y_MLP[1] + 8 * (GROUPS - 1) + 2 * b + half + 1)
                root(NORM_OUT, b)

        @block.vector
        def _(dve):
            self_at = [0]

            def link(ins, base=0):
                self_at[0] += 1
                ins.then_inc(dve_self, 1)
                dve.wait_ge(dve_self, base + self_at[0])

            def rms(n, b, halves, meanwhile=None):
                total, rt, t = col(1, n, b), col(2, n, b), col(3, n, b)
                if halves:
                    dve.wait_ge(sq_ok, SQUARES[n] + 2 * b + 2)
                    ms = nc.vector.tensor_scalar(total, col(0, n, b), col(4, n, b), D * EPS, ALU.add, ALU.add)
                else:
                    dve.wait_ge(sq_ok, SQUARES[n] + b + 1)
                    ms = nc.vector.tensor_scalar(total, col(0, n, b), D * EPS, None, ALU.add)
                ms.then_inc(ms_ok, 1)
                if meanwhile:
                    meanwhile()
                dve.wait_ge(ms_ok, 4 * n + b + 1)
                dve.wait_ge(root_ok, 4 * n + b + 1)
                link(nc.vector.reciprocal(rt, rt))
                link(nc.vector.scalar_tensor_tensor(t, rt, rt, total, ALU.mult, ALU.mult))
                link(nc.vector.tensor_scalar(t, t, -0.5 / D, 1.5, ALU.mult, ALU.add))
                link(nc.vector.tensor_tensor(rinv[:, 4 * n + b:4 * n + b + 1], rt, t, ALU.mult))

            def normed(n, b, dst, done):
                nc.vector.scalar_tensor_tensor(dst, h[:, b, :], rinv[:, 4 * n + b:4 * n + b + 1], gain[:, 0, :],
                                               ALU.mult, ALU.mult).then_inc(done, 1)

            def act_low(gen, b, src=None):
                dve.wait_ge(act_hi_ok, 4 * gen + b + 1)
                at = slice(b * P, (b + 1) * P)
                nc.vector.tensor_tensor(act_lo[:, :, at], turn_banks(gen, b) if src is None else src,
                                        act_hi[:, :, at].bitcast(F32), ALU.subtract).then_inc(act_lo_ok, 1)

            def cw_low(e, s):
                dve.wait_ge(cw_hi_ok, e + 1)
                nc.vector.tensor_tensor(cw_lo[:, s], cw_raw[:, s], cw_hi[:, s].bitcast(F32),
                                        ALU.subtract).then_inc(cw_lo_ok, 1)

            def cw_low_half(a, ready, done):
                dve.wait_ge(ready, 1)
                nc.vector.tensor_tensor(cw_lo[:, 0, :, a, :], cw_raw[:, 0, :, a, :], cw_hi[:, 0, :, a, :].bitcast(F32),
                                        ALU.subtract).then_inc(done, 1)

            nc.vector.memset(stats[:, 4, 38:39], 1.0).then_inc(stats_ok, 1)
            for b in range(NB):
                rms(NORM_X, b, False)
                if b == 0:
                    dve.wait_ge(gain_in[0], 16)
                if b >= 2:
                    dve.wait_ge(turned, b - 1)
                normed(NORM_X, b, tok[:, b % 2, :], tok_ok)
                if b == 0:
                    dve.wait_ge(par_t, 1)
                    nc.vector.tensor_copy(params[:, :, 0:NPAR],
                                          ps[:, 7, 0:NC * NPAR].rearrange("p (c k) -> p c k", c=NC)).then_inc(par_ok, 1)
                if b == 1:
                    act_low(GEN_X, 0)
                    cw_low_half(0, cw_half_hi, cw_half_lo)
                    act_low(GEN_X, 1)
                    cw_low_half(1, cw_hi_ok, cw_lo_ok)
            act_low(GEN_X, 2)
            dve.wait_ge(par_ok, 1)
            dve.wait_ge(par_hi_ok, 1)
            link(nc.vector.tensor_copy(params[:, :, NPAR:NPAR + LAST_TAPS], par_r.bitcast(F32)))
            link(nc.vector.tensor_tensor(params[:, :, NPAR + LAST_TAPS:NCUR], params[:, :, 0:LAST_TAPS],
                                         par_r.bitcast(F32), ALU.subtract))
            act_low(GEN_X, 3)
            cw_low(1, 1)

            def current(e, s, again=True):
                if again:
                    dve.wait_ge(diag_ok, e - 1)
                nc.vector.tensor_copy(par[:, s, :], params[:, bass.ds(e, 1), :]).then_inc(cur_ok, 1)

            def add_taps(e, s):
                dve.wait_ge(taps_ok, e + 1)
                nc.vector.tensor_tensor(relu[:, s, :], relu[:, s, :], ps[:, 4 + s, :], ALU.add).then_inc(conv_ok, 1)

            def conv_chunk(e, s, again=True, more=True, after=True, base=0, others=PE_TAPS, meanwhile=None, finish=True):
                dve.wait_ge(cur_ok, e + 1)
                dve.wait_ge(sig_ok, e + 1)
                nc.vector.scalar_tensor_tensor(upad[:, s, PAD:], ps[:, 2 * s, :], par[:, s, TAPS + 1:TAPS + 2],
                                               relu[:, s, :], ALU.add, ALU.mult).then_inc(glu_ok, 1)
                dve.wait_ge(glu_ok, e + 1)
                sums = (relu[:, s, :], odd_sum[:])
                for n, t in enumerate(range(others, TAPS)):
                    window, weight = upad[:, s, t:t + S], par[:, s, t:t + 1]
                    if n == 2:
                        dve.wait_ge(up_hi_ok, e + 1)
                        nc.vector.tensor_tensor(upad_lo[:, s], upad[:, s], upad_hi[:, s].bitcast(F32),
                                                ALU.subtract).then_inc(up_lo_ok, 1)
                    if n >= 2:
                        dve.wait_ge(dve_self, base + (self_at[0] - 1))
                    if n == 0:
                        step = nc.vector.tensor_scalar(sums[0], window, weight, par[:, s, TAPS:TAPS + 1],
                                                       ALU.mult, ALU.add)
                    elif n == 1:
                        step = nc.vector.tensor_scalar(sums[1], window, weight, None, ALU.mult)
                    else:
                        step = nc.vector.scalar_tensor_tensor(sums[n % 2], window, weight, sums[n % 2],
                                                              ALU.mult, ALU.add)
                    self_at[0] += 1
                    step.then_inc(dve_self, 1)
                    if n == 3 and after:
                        current(e + 1, 1 - s, again or s == 1)
                    if n == 8 and meanwhile:
                        meanwhile()
                    if n == 8 and more:
                        cw_low(e + 2, s)
                dve.wait_ge(dve_self, base + self_at[0])
                link(nc.vector.tensor_tensor(sums[0], sums[0], sums[1], ALU.add), base)
                if finish:
                    add_taps(e, s)

            dve.wait_ge(setup, 2)
            current(0, 0, False)
            conv_chunk(0, 0, False)
            conv_chunk(1, 1, False)
            per_pair = 2 * (TAPS - PE_TAPS + 1)
            with dve.Fori(0, 2) as i:
                for s in range(2):
                    conv_chunk(2 * i + (2 + s), s, base=per_pair * i)
            self_at[0] += per_pair
            conv_chunk(6, 0, more=False, others=LAST_TAPS, finish=False)
            conv_chunk(7, 1, more=False, after=False, others=LAST_TAPS, meanwhile=lambda: add_taps(6, 0))

            for half in range(2):
                dve.wait_ge(ctok_ok, (half + 1) * NC // 2)
                for b in range(NB):
                    last = nc.vector.bn_stats(bn[:, b, half, :], ctok[:, b, half * 512:(half + 1) * 512])
            link(last)
            for b in range(NB):
                last = nc.vector.bn_aggr(moments[:, b, :], bn[:, b].rearrange("p a k -> p (a k)"))
            link(last)
            ln = slice(32, 36)
            nc.vector.tensor_scalar(stats[:, 1, ln], moments[:, :, 1], 1.0, EPS, ALU.mult, ALU.add).then_inc(bn_ok, 1)
            dve.wait_ge(gain_in[0], 32)
            dve.wait_ge(gain_in[1], 16)

            def center(b):
                if b >= 2:
                    dve.wait_ge(turned, 4 * GEN_LN + b - 1)
                link(nc.vector.scalar_tensor_tensor(tok[:, b % 2, :], ctok[:, b, :], moments[:, b, 0:1], gain[:, 0, :],
                                                    ALU.subtract, ALU.mult))

            def swish(b):
                dve.wait_ge(swish_sig, b + 1)
                nc.vector.tensor_tensor(tok[:, b % 2, :], tok[:, b % 2, :], spare, ALU.mult).then_inc(tok_ok, 1)

            center(0)
            rt, t = stats[:, 2, ln], stats[:, 3, ln]
            dve.wait_ge(lnroot_ok, 1)
            link(nc.vector.reciprocal(rt, rt))
            link(nc.vector.tensor_tensor(t, rt, rt, ALU.mult))
            link(nc.vector.tensor_tensor(t, t, stats[:, 1, ln], ALU.mult))
            link(nc.vector.tensor_scalar(t, t, -0.5, 1.5, ALU.mult, ALU.add))
            link(nc.vector.tensor_tensor(rinv[:, ln], rt, t, ALU.mult))
            halves = (slice(0, 512), slice(512, 1024))
            for at, done in zip(halves, (y_half, y_ok)):
                nc.vector.scalar_tensor_tensor(tok[:, 0, at], tok[:, 0, at], rinv[:, 32:33], gain[:, 1, at],
                                               ALU.mult, ALU.add).then_inc(done, 1)
            for at, ready, done in zip(halves, (sig_half, swish_sig), (tok_half, tok_ok)):
                dve.wait_ge(ready, 1)
                nc.vector.tensor_tensor(tok[:, 0, at], tok[:, 0, at], spare[:, at], ALU.mult).then_inc(done, 1)
            center(1)
            banks = turn_banks(GEN_LN, 0)
            for cs, ready, count, done in ((slice(0, NC // 2), act_half_hi, 1, act_half_lo),
                                           (slice(NC // 2, NC), act_hi_ok, 4 * GEN_LN + 1, act_lo_ok)):
                dve.wait_ge(ready, count)
                nc.vector.tensor_tensor(act_lo[:, cs, 0:P], banks[:, cs], act_hi[:, cs, 0:P].bitcast(F32),
                                        ALU.subtract).then_inc(done, 1)
            for b in range(1, NB):
                nc.vector.scalar_tensor_tensor(tok[:, b % 2, :], tok[:, b % 2, :], rinv[:, 32 + b:33 + b],
                                               gain[:, 1, :], ALU.mult, ALU.add).then_inc(y_ok, 1)
                if b < 3:
                    center(b + 1)
                if b >= 2:
                    act_low(GEN_LN, b - 1)
                swish(b)
            act_low(GEN_LN, 3)

            def add_tile(n, b, half, bank):
                dve.wait_ge(y_done, n + 1)
                at = h[:, b, half * 512:(half + 1) * 512]
                nc.vector.tensor_tensor(at, at, bank, ALU.add).then_inc(y_added, 1)

            def w1_low(n, j):
                dve.wait_ge(w1_hi_ok, n + 1)
                nc.vector.tensor_tensor(m1_lo[:, j], m1_raw[:, j], m1_hi[:, j].bitcast(F32),
                                        ALU.subtract).then_inc(w1_lo_ok, 1)

            dve.wait_ge(b2_in, 16)
            for b in range(NB):
                link(nc.vector.tensor_tensor(h[:, b, :], h[:, b, :], b2, ALU.add))
                add_tile(b, b, 0, ps[:, b, :])
            for b in range(NB):
                add_tile(4 + b, b, 1, ps[:, 4 + b, :])
                rms(NORM_MLP0, b, True, (lambda k=b - 1: act_low(GEN_MLP0, k)) if b else None)
                if b == 0:
                    dve.wait_ge(gain_in[0], 48)
                if b >= 2:
                    dve.wait_ge(turned, 4 * GEN_MLP0 + b - 1)
                normed(NORM_MLP0, b, tok[:, b % 2, :], tok_ok)
                if b < 3:
                    w1_low(b, b)
            w1_low(3, 3)
            act_low(GEN_MLP0, 3)
            def w2_low(n, j):
                dve.wait_ge(w2_hi_ok, n + 1)
                nc.vector.tensor_tensor(m2_lo[:, j], m2_raw[:, j], m2_hi[:, j].bitcast(F32),
                                        ALU.subtract).then_inc(w2_lo_ok, 1)

            def mlp_up(layer, g, first=False):
                if first:
                    for j in range(GF):
                        w2_low(4 * g + (32 * layer + j), j)
                for j in range(GF):
                    n = 4 * g + (32 * layer + j)
                    dve.wait_ge(relu_ok, n + 1)
                    nc.vector.tensor_tensor(relu[:, j % 2, :], relu[:, j % 2, :], relu[:, j % 2, :],
                                            ALU.mult).then_inc(usq_ok, 1)
                    if not first:
                        w2_low(n, j)
                    dve.wait_ge(u_hi_ok, n + 1)
                    nc.vector.tensor_tensor(u_lo[:, j], relu[:, j % 2, :], u_hi[:, j].bitcast(F32),
                                            ALU.subtract).then_inc(u_lo_ok, 1)

            def mlp_add(layer, g, q):
                add_tile(8 * g + (Y_MLP[layer] + q), q // 2, q % 2, mlp_bank(q))

            def mlp_group(layer, g, first=False):
                mlp_up(layer, g, first)
                for q in range(NQ):
                    if q in (0, 2, 4, 6):
                        w1_low(4 * g + (32 * layer + 4 + q // 2), q // 2)
                    mlp_add(layer, g, q)

            mlp_group(0, 0, True)
            with dve.Fori(1, GROUPS - 1) as g:
                mlp_group(0, g)
            dve.wait_ge(band_ok, 1)
            nc.vector.reciprocal(inv_first[:], inv_first[:])
            dve.wait_ge(pw_hi_ok, 1)
            nc.vector.tensor_tensor(pw_lo[:], pw_raw, pw_hi[:].bitcast(F32), ALU.subtract).then_inc(pw_lo_ok, 1)
            mlp_up(0, GROUPS - 1)

            w1_low(32, 0)

            def pt_low(b):
                dve.wait_ge(pt_hi_ok, b + 1)
                nc.vector.tensor_tensor(pt_lo[:, 1 + b % 3], tok[:, 0, :], pt_hi[:, 1 + b % 3].bitcast(F32),
                                        ALU.subtract).then_inc(pt_lo_ok, 1)

            for b in range(NB):
                mlp_add(0, GROUPS - 1, 2 * b)
                mlp_add(0, GROUPS - 1, 2 * b + 1)
                if b == 2:
                    dve.wait_ge(turned, 4 * GEN_POOL + 1)
                    for k in range(2):
                        src = turn_banks(GEN_POOL, 0).rearrange("p (g k) t -> p g k t", k=2)[:, :, k, :]
                        dst = spare.rearrange("p (g k t) -> p g k t", k=2, t=P)[:, :, k, :]
                        last = nc.vector.tensor_tensor(dst, src, inv_first[:], ALU.mult)
                    last.then_inc(pooled_ok, 1)
                if b:
                    pt_low(b - 1)
                rms(NORM_POOL, b, True)
                if b == 0:
                    dve.wait_ge(gain_in[0], 64)
                else:
                    dve.wait_ge(pt_lo_ok, b)
                normed(NORM_POOL, b, tok[:, 0, :], tok_ok)
                if b == 2:
                    act_low(GEN_POOL, 0, spare.rearrange("p (c t) -> p c t", t=P))
                if b == 3:
                    act_low(GEN_POOL, 1)
            pt_low(3)
            act_low(GEN_POOL, 2)

            def add_pool(b):
                dve.wait_ge(y_done, Y_POOL + b + 1)
                dve.wait_ge(pb_added, b + 1)
                lo = 2 * (b % 2)
                at = h[:, b, :].rearrange("p (k d) -> p k d", k=2)
                nc.vector.tensor_tensor(at, at, ps[:, lo:lo + 2, :], ALU.add).then_inc(y_added, 1)

            def between(b):
                if b < 3:
                    add_pool(b + 1)
                if b == 2:
                    act_low(GEN_MLP1, 1)

            add_pool(0)
            for b in range(NB):
                rms(NORM_MLP1, b, False, lambda k=b: between(k))
                if b == 0:
                    dve.wait_ge(gain_in[0], 80)
                if b == 1:
                    dve.wait_ge(pb_added, NB)
                if b >= 2:
                    dve.wait_ge(turned, 4 * GEN_MLP1 + b - 1)
                normed(NORM_MLP1, b, tok[:, b % 2, :], tok_ok)
                if b == 0:
                    act_low(GEN_POOL, 3)
                if b == 1:
                    act_low(GEN_MLP1, 0)
                if b == 2:
                    w1_low(33, 1)
            w1_low(34, 2)
            w1_low(35, 3)
            act_low(GEN_MLP1, 2)
            act_low(GEN_MLP1, 3)

            mlp_group(1, 0, True)
            with dve.Fori(1, GROUPS - 1) as g:
                mlp_group(1, g)
            mlp_up(1, GROUPS - 1)

            def store_tile(b):
                if b == 0:
                    dve.wait_ge(gain_in[0], 96)
                if b >= 2:
                    dve.wait_ge(stored[b % 2], 32)
                for k in range(2):
                    at = slice(k * 512, (k + 1) * 512)
                    nc.vector.scalar_tensor_tensor(tok[:, b % 2, at], h[:, b, at],
                                                   rinv[:, 4 * NORM_OUT + b:4 * NORM_OUT + b + 1], gain[:, 0, at], ALU.mult, ALU.mult).then_inc(out_ok, 1)

            def before_root(b):
                if b >= 1:
                    store_tile(b - 1)
                if b < 3:
                    mlp_add(1, GROUPS - 1, 2 * b + 2)

            mlp_add(1, GROUPS - 1, 0)
            for b in range(NB):
                mlp_add(1, GROUPS - 1, 2 * b + 1)
                rms(NORM_OUT, b, True, lambda k=b: before_root(k))
            store_tile(NB - 1)

        @block.tensor
        def _(pe):
            def product(dst, left, right, n, count):
                (lh, ll), (rh, rl) = left, right
                nc.tensor.matmul(dst, lh, rh, start=(n == 0), stop=False)
                nc.tensor.matmul(dst, lh, rl, start=False, stop=False)
                return nc.tensor.matmul(dst, ll, rh, start=False, stop=(n == count - 1))

            def act_tile(c, at):
                return act_hi[:, c, at], act_lo[:, c, at]

            def block_cols(b):
                return slice(b * P, (b + 1) * P)

            def turn(gen, b, src):
                pe.wait_ge(tok_ok, 4 * gen + b + 1)
                if b >= 2:
                    pe.wait_ge(act_lo_ok, 4 * gen + b - 1)
                banks = turn_banks(gen, b)
                for c in range(NC):
                    last = nc.tensor.transpose(banks[:, c, :], src[:, c * P:(c + 1) * P], ident[:])
                last.then_inc(turned, 1)

            pe.wait_ge(ident_ok, 1)
            pe.wait_ge(par_in, 48)
            for c in range(NC):
                last = nc.tensor.transpose(ps[:, 7, c * NPAR:(c + 1) * NPAR], par_rows[:, c * P:(c + 1) * P],
                                           ident[0:NPAR, 0:NPAR])
            last.then_inc(par_t, 1)

            def keep_clock(count):
                for _ in range(count):
                    nc.tensor.transpose(ps[:, 3, 0:P], ident[:], ident[:])

            def keep_clock_long(count, left, right):
                for _ in range(count):
                    nc.tensor.matmul(ps[:, 0, :], left, right, start=True, stop=True)

            keep_clock(4)
            turn(GEN_X, 0, tok[:, 0, :])
            keep_clock(12)
            pe.wait_ge(par_ok, 1)
            turn(GEN_X, 1, tok[:, 1, :])

            def glu_product(e, s, again=True):
                pe.wait_ge(cw_lo_ok, e + 1)
                if again:
                    pe.wait_ge(glu_ok, e - 1)
                for a in range(2):
                    for c in range(NC):
                        last = product(ps[:, 2 * s + a, :], (cw_hi[:, s, c, a, :], cw_lo[:, s, c, a, :]),
                                       act_tile(c, slice(0, S)), c, NC)
                last.then_inc(glu_mm, 1)

            def taps(e, s, again, count=PE_TAPS):
                pe.wait_ge(diag_ok, e + 1)
                pe.wait_ge(up_lo_ok, e + 1)
                if again:
                    pe.wait_ge(conv_ok, e - 1)
                for t in range(count):
                    last = product(ps[:, 4 + s, :], (diag_hi[:, s, t], diag_lo[:, s, t]),
                                   (upad_hi[:, s, t:t + S], upad_lo[:, s, t:t + S]), t, count)
                last.then_inc(taps_ok, 1)

            def conv_turn(e, s, again=True):
                pe.wait_ge(conv_ok, e + 1)
                if again:
                    pe.wait_ge(ctok_ok, e)
                for b in range(NB):
                    last = nc.tensor.transpose(ps[:, 6 + s, block_cols(b)], relu[:, s, block_cols(b)], ident[:])
                last.then_inc(conv_turned, 1)

            keep_clock(16)
            pe.wait_ge(act_lo_ok, 2)
            pe.wait_ge(cw_half_lo, 1)
            for pair in range(2):
                cols = slice(pair * 2 * P, (pair + 1) * 2 * P)
                if pair:
                    pe.wait_ge(act_lo_ok, NB)
                for a in range(2):
                    if a and not pair:
                        pe.wait_ge(cw_lo_ok, 1)
                    for c in range(NC):
                        last = product(ps[:, a, cols], (cw_hi[:, 0, c, a, :], cw_lo[:, 0, c, a, :]),
                                       act_tile(c, cols), c, NC)
                        if pair == 0 and c == (NC - 1, NC // 2 - 1)[a]:
                            turn(GEN_X, 2 + a, tok[:, a, :])
            last.then_inc(glu_mm, 1)
            glu_product(1, 1, False)
            taps(0, 0, False)
            glu_product(2, 0)
            taps(1, 1, False)
            conv_turn(0, 0, False)
            with pe.Fori(0, 2) as i:
                for s in range(2):
                    glu_product(2 * i + (3 + s), 1 - s)
                    taps(2 * i + (2 + s), s, True)
                    conv_turn(2 * i + (1 + s), 1 - s)
            glu_product(7, 1)
            conv_turn(5, 1)
            pe.wait_ge(diag_more_ok, 1)
            taps(6, 0, True, LAST_TAPS)
            taps(7, 1, True, LAST_TAPS)
            conv_turn(6, 0)
            conv_turn(7, 1)

            def conv_out(b, half, bank, at=0, between=None):
                for c in range(NC):
                    if c == at and between:
                        between()
                    if b == 0 and half == 0 and c == NC // 2:
                        pe.wait_ge(act_lo_ok, 4 * GEN_LN + 1)
                    last = product(ps[:, bank, :], act_tile(c, block_cols(b)), (c2_hi[half][:, c, :], c2_lo[half][:, c, :]),
                                   c, NC)
                last.then_inc(y_done, 1)

            keep_clock_long(38, act_hi[:, 0, 0:P], act_hi[:, 1, :])
            banks = turn_banks(GEN_LN, 0)
            for k in range(2):
                if k == 0:
                    pe.wait_ge(tok_half, 1)
                else:
                    pe.wait_ge(tok_ok, 4 * GEN_LN + 1)
                for c in range(k * NC // 2, (k + 1) * NC // 2):
                    last = nc.tensor.transpose(banks[:, c, :], tok[:, 0, c * P:(c + 1) * P], ident[:])
                last.then_inc(turned_half if k == 0 else turned, 1)
            for b in range(NB):
                if b == 0:
                    pe.wait_ge(act_half_lo, 1)
                    pe.wait_ge(c2_lo_ok, 1)
                else:
                    pe.wait_ge(act_lo_ok, 4 * GEN_LN + b + 1)
                conv_out(b, 0, b, NC // 2 + (NC // 4 if b == 0 else 0),
                         (lambda k=b + 1: turn(GEN_LN, k, tok[:, k % 2, :])) if b < NB - 1 else None)
            pe.wait_ge(c2_lo_ok, 2)
            for b in range(NB):
                conv_out(b, 1, 4 + b, NC // 4, (lambda k=b - 2: turn(GEN_MLP0, k, tok[:, k % 2, :])) if b >= 2 else None)

            def mlp_up(layer, g):
                for j in range(GF):
                    n = 4 * g + (32 * layer + j)
                    pe.wait_ge(w1_lo_ok, n + 1)
                    pe.wait_ge(y_added, 8 * g + (Y_MLP[layer] - 3 + j))
                    for c in range(NC):
                        last = product(ps[:, j, :], (m1_hi[:, j, c, :], m1_lo[:, j, c, :]), act_tile(c, slice(0, S)), c, NC)
                    last.then_inc(up_mm, 1)

            def mlp_up_first(layer, gen):
                for pair in range(2):
                    cols = slice(pair * 2 * P, (pair + 1) * 2 * P)
                    pe.wait_ge(act_lo_ok, 4 * gen + 2 * pair + 2)
                    for j in range(GF):
                        if pair == 0:
                            pe.wait_ge(w1_lo_ok, 32 * layer + j + 1)
                        for c in range(NC):
                            last = product(ps[:, j, cols], (m1_hi[:, j, c, :], m1_lo[:, j, c, :]), act_tile(c, cols), c, NC)
                        if pair:
                            last.then_inc(up_mm, 1)
                        elif j % 2 == 0:
                            turn(gen, 2 + j // 2, tok[:, j // 2, :])

            def down_tile(q, feats, done=False):
                b, half = q // 2, q % 2
                for f in feats:
                    last = product(mlp_bank(q), (u_hi[:, f, block_cols(b)], u_lo[:, f, block_cols(b)]),
                                   (m2_hi[:, f, half * 512:(half + 1) * 512], m2_lo[:, f, half * 512:(half + 1) * 512]), f, GF)
                if done:
                    last.then_inc(y_done, 1)

            def mlp_down(layer, g, between=None):
                n = 4 * g + 32 * layer
                pe.wait_ge(w2_lo_ok, n + 3)
                pe.wait_ge(u_lo_ok, n + 3)
                for q in range(4):
                    down_tile(q, range(GF - 1))
                pe.wait_ge(w2_lo_ok, n + 4)
                pe.wait_ge(u_lo_ok, n + 4)
                for q in range(4):
                    down_tile(q, [GF - 1], True)
                for q in range(4, NQ):
                    down_tile(q, range(GF), True)
                    if q == 5 and between:
                        between()

            mlp_up_first(0, GEN_MLP0)
            mlp_down(0, 0)
            with pe.Fori(1, GROUPS - 1) as g:
                mlp_up(0, g)
                mlp_down(0, g)
            mlp_up(0, GROUPS - 1)

            def pool_turn(b):
                pe.wait_ge(pt_lo_ok, b + 1)
                if b >= 2:
                    pe.wait_ge(act_lo_ok, 4 * GEN_POOL + b - 1)
                banks = turn_banks(GEN_POOL, b)
                own, before = 1 + b % 3, 1 + (b - 1) % 3
                matrix = band0 if b == 0 else band
                for c in range(NC):
                    g, at = c // 2, slice(c * P, (c + 1) * P)
                    nc.tensor.matmul(banks[:, c, :], pt_hi[:, own, at], matrix[:, g, :], start=True, stop=False)
                    last = nc.tensor.matmul(banks[:, c, :], pt_lo[:, own, at], matrix[:, g, :], start=False, stop=(b == 0))
                    if b:
                        nc.tensor.matmul(banks[:, c, 0:16], pt_hi[:, before, at], band_prev[:, g, :],
                                         start=False, stop=False)
                        last = nc.tensor.matmul(banks[:, c, 0:16], pt_lo[:, before, at], band_prev[:, g, :],
                                                start=False, stop=True)
                last.then_inc(turned, 1)

            def pool_product(b):
                pe.wait_ge(act_lo_ok, 4 * GEN_POOL + b + 1)
                if b == 0:
                    pe.wait_ge(pw_lo_ok, 1)
                    pe.wait_ge(y_added, Y_POOL)
                if b >= 2:
                    pe.wait_ge(y_added, Y_POOL + b - 1)
                for g in range(NG):
                    dst = ps[:, 2 * (b % 2) + g // 2, (g % 2) * 256:(g % 2 + 1) * 256]
                    for k in range(2):
                        last = product(dst, act_tile(2 * g + k, block_cols(b)),
                                       (pw_hi[:, 2 * g + k, :], pw_lo[:, 2 * g + k, :]), k, 2)
                last.then_inc(y_done, 1)

            mlp_down(0, GROUPS - 1, lambda: pool_turn(0))
            pool_turn(1)
            pool_product(0)
            pool_turn(2)
            pool_product(1)
            pool_turn(3)
            pool_product(2)
            turn(GEN_MLP1, 0, tok[:, 0, :])
            pool_product(3)
            turn(GEN_MLP1, 1, tok[:, 1, :])
            pe.wait_ge(y_added, Y_POOL + 3)
            keep_clock_long(9, pw_hi[:, 0, 0:P], pw_hi[:, 0:2, :])
            mlp_up_first(1, GEN_MLP1)
            mlp_down(1, 0)
            with pe.Fori(1, GROUPS - 1) as g:
                mlp_up(1, g)
                mlp_down(1, g)
            mlp_up(1, GROUPS - 1)
            mlp_down(1, GROUPS - 1)


_INS = ["x", "norm_mix", "norm_mlp", "conv_w1", "conv_b1", "conv_dw", "conv_dwb", "conv_ln_g", "conv_ln_b",
        "conv_w2", "conv_b2", "pool_w", "pool_b", "pool_scale", "mlp_w1", "mlp_w2", "final_norm"]


def kernel(**inputs):
    import numpy as _np
    import concourse.bacc as _bacc
    from concourse import mybir as _mybir
    from concourse.bass_utils import run_bass_kernel_spmd as _run

    nc = _bacc.Bacc("TRN2", target_bir_lowering=False, num_devices=1)
    arrays, args = {}, []
    for name in _INS:
        a = _np.ascontiguousarray(inputs[name])
        arrays[f"in_{name}"] = a
        args.append(nc.dram_tensor(f"in_{name}", a.shape, _mybir.dt.from_np(a.dtype), kind="ExternalInput").ap())
    out = nc.dram_tensor("out", (1, S, D), F32, kind="ExternalOutput").ap()
    hybrid_encoder(nc, *args, out)
    return _run(nc, [arrays], core_ids=[0]).results[0]["out"]
```
